# Optimizing a Trainium2 kernel written in Bass

```python
import jax, jax.numpy as jnp
from jax import lax
import numpy as np

D_MODEL = 1024
BATCH = 1
SEQ = 2048
DEPTH = 1
DEC_BATCH = 1
DEC_SEQ = 32
PAST_LEN = 2048

CHUNK = 64
LEFT_CHUNKS = 8
BAND = (LEFT_CHUNKS + 1) * CHUNK
ATTN_WIDTH = D_MODEL // 2
N_HEADS = 8
HEAD_DIM = ATTN_WIDTH // N_HEADS
CONV_WIDTH = D_MODEL - ATTN_WIDTH
CONV_KERNEL = 31
REL_CLIP = 128
N_REL = 2 * REL_CLIP + 1
D_FF = -(-8 * D_MODEL // (3 * 256)) * 256
D_IN = 3 * ATTN_WIDTH + 2 * CONV_WIDTH
RMS_EPS = 1e-6
LN_EPS = 1e-5
NEG_INF = -1e30

kernel_name = "hymba_style_streaming_conformer_step"

def rmsnorm(x, g):
    xf = x.astype(jnp.float32)
    y = xf * lax.rsqrt(jnp.mean(xf * xf, axis=-1, keepdims=True) + RMS_EPS)
    return (y * g.astype(jnp.float32)).astype(x.dtype)

def layernorm(x, g, b):
    xf = x.astype(jnp.float32)
    mu = jnp.mean(xf, axis=-1, keepdims=True)
    xc = xf - mu
    y = xc * lax.rsqrt(jnp.mean(xc * xc, axis=-1, keepdims=True) + LN_EPS)
    return (y * g.astype(jnp.float32) + b.astype(jnp.float32)).astype(x.dtype)

def rel_bias(table, q_idx, k_idx, offset):
    rel = q_idx[:, None] - k_idx[None, :] + offset
    return table[:, jnp.clip(rel, -REL_CLIP, REL_CLIP) + REL_CLIP]

def chunk_attend(q, k, v, bias, key_valid):
    s = jnp.einsum('bnqhd,bnkhd->bnhqk', q, k).astype(jnp.float32) * (HEAD_DIM ** -0.5)
    s = s + bias.astype(jnp.float32)[None, None]
    if key_valid is not None:
        s = jnp.where(key_valid[None, :, None, None, :], s, NEG_INF)
    p = jax.nn.softmax(s, axis=-1).astype(v.dtype)
    return jnp.einsum('bnhqk,bnkhd->bnqhd', p, v)

def band_attention_prompt(q, k, v, table):
    B, S, H, Dh = q.shape
    nc = S // CHUNK
    pad = LEFT_CHUNKS * CHUNK
    kp = jnp.pad(k, ((0, 0), (pad, 0), (0, 0), (0, 0)))
    vp = jnp.pad(v, ((0, 0), (pad, 0), (0, 0), (0, 0)))
    idx = (jnp.arange(nc) * CHUNK)[:, None] + jnp.arange(BAND)[None, :]
    kb = kp[:, idx]
    vb = vp[:, idx]
    bias = rel_bias(table, jnp.arange(CHUNK), jnp.arange(BAND), pad)
    key_valid = idx >= pad
    o = chunk_attend(q.reshape(B, nc, CHUNK, H, Dh), kb, vb, bias, key_valid)
    return o.reshape(B, S, H * Dh)

def band_attention_sample(q, k, v, cache_k, cache_v, table):
    B, T, H, Dh = q.shape
    W = cache_k.shape[1]
    k_all = jnp.concatenate([cache_k, k], axis=1)
    v_all = jnp.concatenate([cache_v, v], axis=1)
    bias = rel_bias(table, jnp.arange(T), jnp.arange(W + T), W)
    o = chunk_attend(q[:, None], k_all[:, None], v_all[:, None], bias, None)
    return o.reshape(B, T, H * Dh), k_all[:, -W:], v_all[:, -W:]

def conformer_conv(u_glu, conv_past, w_dw, b_dw, ln_g, ln_b):
    a, g = jnp.split(u_glu, 2, axis=-1)
    u = a * jax.nn.sigmoid(g)
    buf = jnp.concatenate([conv_past.astype(u.dtype), u], axis=1)
    y = lax.conv_general_dilated(buf, w_dw[:, None, :].astype(u.dtype), (1,), 'VALID',
                                 dimension_numbers=('NWC', 'WIO', 'NWC'),
                                 feature_group_count=CONV_WIDTH) + b_dw
    y = jax.nn.silu(layernorm(y, ln_g, ln_b))
    return y, buf[:, -(CONV_KERNEL - 1):]

def trunk_layer(x, kv_past, conv_past, g_mix, w_in, rel_table, w_dw, b_dw, ln_g, ln_b,
                w_out, g_ffn, w_gate, w_up, w_down):
    B, T, _ = x.shape
    z = rmsnorm(x, g_mix) @ w_in
    q, k, v, u = jnp.split(z, [ATTN_WIDTH, 2 * ATTN_WIDTH, 3 * ATTN_WIDTH], axis=-1)
    q = q.reshape(B, T, N_HEADS, HEAD_DIM)
    k = k.reshape(B, T, N_HEADS, HEAD_DIM)
    v = v.reshape(B, T, N_HEADS, HEAD_DIM)
    if kv_past is None:
        o_attn = band_attention_prompt(q, k, v, rel_table)
        w_keep = min(LEFT_CHUNKS * CHUNK, T)
        new_k, new_v = k[:, -w_keep:], v[:, -w_keep:]
        conv_past = jnp.zeros((B, CONV_KERNEL - 1, CONV_WIDTH), u.dtype)
    else:
        o_attn, new_k, new_v = band_attention_sample(q, k, v, kv_past[0], kv_past[1], rel_table)
    o_conv, new_conv = conformer_conv(u, conv_past, w_dw, b_dw, ln_g, ln_b)
    x = x + jnp.concatenate([o_attn, o_conv], axis=-1) @ w_out
    h = rmsnorm(x, g_ffn)
    x = x + (jax.nn.silu(h @ w_gate) * (h @ w_up)) @ w_down
    return x, new_k, new_v, new_conv

def setup_inputs(seed: int = 0) -> dict:
    key = jax.random.key(seed)
    ks = jax.random.split(key, 20)
    f32 = jnp.float32
    nrm = lambda k, shape, scale: jax.random.normal(k, shape, f32) * scale
    w_past = min(LEFT_CHUNKS * CHUNK, PAST_LEN)
    return {
        "x_prompt": nrm(ks[0], (BATCH, SEQ, D_MODEL), 1.0),
        "x_sample": nrm(ks[1], (DEC_BATCH, DEC_SEQ, D_MODEL), 1.0),
        "cache_k": nrm(ks[2], (DEPTH, DEC_BATCH, w_past, N_HEADS, HEAD_DIM), 1.0),
        "cache_v": nrm(ks[3], (DEPTH, DEC_BATCH, w_past, N_HEADS, HEAD_DIM), 1.0),
        "state_conv": nrm(ks[4], (DEPTH, DEC_BATCH, CONV_KERNEL - 1, CONV_WIDTH), 1.0),
        "g_mix": 1.0 + nrm(ks[5], (DEPTH, D_MODEL), 0.02),
        "w_in": nrm(ks[6], (DEPTH, D_MODEL, D_IN), D_MODEL ** -0.5),
        "rel_table": nrm(ks[7], (DEPTH, N_HEADS, N_REL), 0.1),
        "w_dw": nrm(ks[8], (DEPTH, CONV_KERNEL, CONV_WIDTH), CONV_KERNEL ** -0.5),
        "b_dw": nrm(ks[9], (DEPTH, CONV_WIDTH), 0.02),
        "ln_g": 1.0 + nrm(ks[10], (DEPTH, CONV_WIDTH), 0.02),
        "ln_b": nrm(ks[11], (DEPTH, CONV_WIDTH), 0.02),
        "w_out": nrm(ks[12], (DEPTH, D_MODEL, D_MODEL), D_MODEL ** -0.5),
        "g_ffn": 1.0 + nrm(ks[13], (DEPTH, D_MODEL), 0.02),
        "w_gate": nrm(ks[14], (DEPTH, D_MODEL, D_FF), D_MODEL ** -0.5),
        "w_up": nrm(ks[15], (DEPTH, D_MODEL, D_FF), D_MODEL ** -0.5),
        "w_down": nrm(ks[16], (DEPTH, D_FF, D_MODEL), D_FF ** -0.5),
        "g_final": 1.0 + nrm(ks[17], (D_MODEL,), 0.02),
    }

def reference(x_prompt, x_sample, cache_k, cache_v, state_conv, g_mix, w_in, rel_table,
              w_dw, b_dw, ln_g, ln_b, w_out, g_ffn, w_gate, w_up, w_down, g_final):
    xp, xs = x_prompt, x_sample
    kp_l, vp_l, cp_l, ks_l, vs_l, cs_l = [], [], [], [], [], []
    for l in range(DEPTH):
        params = (g_mix[l], w_in[l], rel_table[l], w_dw[l], b_dw[l], ln_g[l], ln_b[l],
                  w_out[l], g_ffn[l], w_gate[l], w_up[l], w_down[l])
        xp, kp, vp, cp = trunk_layer(xp, None, None, *params)
        xs, kn, vn, cn = trunk_layer(xs, (cache_k[l], cache_v[l]), state_conv[l], *params)
        kp_l.append(kp); vp_l.append(vp); cp_l.append(cp)
        ks_l.append(kn); vs_l.append(vn); cs_l.append(cn)
    y_prompt = rmsnorm(xp, g_final)
    y_sample = rmsnorm(xs, g_final)
    return (y_prompt, y_sample, jnp.stack(kp_l), jnp.stack(vp_l), jnp.stack(cp_l),
            jnp.stack(ks_l), jnp.stack(vs_l), jnp.stack(cs_l))


_drawn_inputs = setup_inputs


def setup_inputs(seed=0):
    import zlib

    import numpy as np

    out = dict(_drawn_inputs(seed))
    spreads = {}
    factors = {'rel_table': 8.0,
     'b_dw': 3.404,
     'ln_g': 5.073,
     'ln_b': 6.289,
     'g_ffn': 3.922,
     'g_final': 2.865}
    for name, (base, spread) in spreads.items():
        noise = np.random.default_rng([zlib.crc32(name.encode()), seed]).standard_normal(out[name].shape)
        drawn = base * np.exp(spread * noise) if base else spread * noise
        out[name] = __import__('jax').numpy.asarray(drawn.astype(out[name].dtype))
    for name, factor in factors.items():
        out[name] = (out[name] * factor).astype(out[name].dtype)
    return out
```

```python
from contextlib import ExitStack

import concourse.bass as bass
from concourse import mybir

F32 = mybir.dt.float32
F32R = mybir.dt.float32r
ALU = mybir.AluOpType
ACT = mybir.ActivationFunctionType
AX_X = mybir.AxisListType.X

P = 128
D = 1024
KD = D // P
SEQ = 2048
TB = 512
NB = SEQ // TB
DEC = 32
W0 = TB + DEC
H = 8
HD = 64
AW = H * HD
FT = AW // P
CHUNK = 64
NPAIR = TB // P
BANDW = 640
FAR = 384
NEAR = BANDW - FAR
CLIP = 128
TAPS = 31
PAST = TAPS - 1
D_FF = 2816
F_CHUNKS = [8, 8, 6]
RMS_EPS = 1e-6
LN_EPS = 1e-5
NEG = -1e30
Q_SCALE = HD ** -0.5

U_IN, U_OUT = 20, 8
UNITS = U_IN + U_OUT + sum(2 * c + KD for c in F_CHUNKS)

STAGES = ["load", "norm_mix", "w_in", "attend", "conv_norm", "w_out", "norm_ffn"]
for c in range(len(F_CHUNKS)):
    STAGES += [f"gate_up{c}", f"down{c}"]
STAGES += ["norm_final", "store"]

C_GMIX, C_GFFN, C_GFIN = 0, 8, 16
C_BDW, C_LNG, C_LNB = 24, 28, 32
C_FARB = 36
C_WDW = 44
C_PAST = C_WDW + FT * TAPS
C_ALL = C_PAST + FT * PAST


def unit_base(b, stage):
    u = UNITS * b
    if stage == "w_in":
        return u
    if stage == "w_out":
        return u + U_IN
    u += U_IN + U_OUT
    c = int(stage[-1])
    u += sum(2 * f + KD for f in F_CHUNKS[:c])
    return u if stage.startswith("gate_up") else u + 2 * F_CHUNKS[c]


def dve_evac_base(b, stage):
    return unit_base(b, stage) - (U_IN - 8) * (b + (stage != "w_in"))


def band_tiles(b, p):
    return [j for j in range(5) if b > 0 or p + j >= NPAIR]


def n_pairs(b):
    return NPAIR + (b == 0)


def n_key_tiles(b):
    return 9 if b == 0 else 8


def build(nc, w_units, x_prompt, x_sample, cache_k, cache_v, consts, rel_near,
          y_prompt, y_sample, nk_prompt, nv_prompt, nc_prompt, nk_sample, nv_sample, nc_sample):
    ctx = ExitStack()
    with ctx:
        def sb(name, shape, dt=F32):
            return ctx.enter_context(nc.sbuf_tensor(name, shape, dt))

        def sem(name):
            return ctx.enter_context(nc.semaphore(name))

        x = sb("x", [P, KD, W0])
        a_hi = sb("a_hi", [P, KD, W0], F32R)
        a_lo = sb("a_lo", [P, KD, W0], F32R)
        kT = sb("kT", [P, FT, 2 * TB + DEC])
        v = sb("v", [P, 2 * NPAIR + 1, AW])
        w_raw = sb("w_raw", [P, 4, D])
        w_hi = sb("w_hi", [P, 2, D], F32R)
        w_lo = sb("w_lo", [P, 2, D], F32R)
        bias = sb("bias", [P, H, NEAR])
        cst = sb("cst", [P, C_ALL])
        rstd = sb("rstd", [P, W0])
        tmp = sb("tmp", [P, 2, W0])
        x_in = sb("x_in", [P, 2, D])
        ident = sb("ident", [P, P])
        ones_d = sb("ones_d", [P, P])
        ones_c = sb("ones_c", [P, P])
        mask_q = sb("mask_q", [P, P], F32R)
        mask_k = sb("mask_k", [P, CHUNK], F32R)
        tail = sb("tail", [P, FT, PAST])
        tail_s = sb("tail_s", [P, FT, PAST])
        small = sb("small", [P, 16])
        tick = sb("tick", [P, 2])

        att_bytes = 4 * (FT * W0 + NPAIR * BANDW + 544 + 4 * TB + 2 * 640 + (2 * TB + DEC) + 9 * P)
        act_bytes = 4 * 2 * F_CHUNKS[0] * W0
        at = [0]

        def reserve(name, n_bytes):
            at[0] = -(-nc.sbuf_base // 32) * 32
            sb(name, [P, n_bytes // 4 + 16])
            return at[0]


        def place(name, shape, dt=F32, start=None):
            if start is not None:
                at[0] = start
            n = 4
            for s in shape[1:]:
                n *= s
            t = nc.alloc_sbuf_tensor_at(name, shape, dt, offset=at[0])
            at[0] += n
            return t

        base = reserve("att_or_ffn", max(att_bytes, act_bytes))
        q = place("q", [P, FT, W0])
        probs = place("probs", [P, NPAIR, BANDW])
        probs_s = place("probs_s", [P, 544])
        pT_hi = place("pT_hi", [P, 2, TB], F32R)
        pT_lo = place("pT_lo", [P, 2, TB], F32R)
        q_hi = place("q_hi", [P, 640], F32R)
        q_lo = place("q_lo", [P, 640], F32R)
        k_st = place("k_st", [P, 2 * TB + DEC], F32R)
        v_st = place("v_st", [P, 9, P], F32R)
        act_hi = place("act_hi", [P, F_CHUNKS[0], W0], F32R, start=base)
        act_lo = place("act_lo", [P, F_CHUNKS[0], W0], F32R)
        UW = PAST + TB + PAST + DEC
        YW = TB + PAST + DEC
        base = reserve("conv_or_rows", 4 * FT * (UW + YW))
        u = place("u", [P, FT, UW])
        y = place("y", [P, FT, YW])
        rows = place("rows", [P, 2, D], start=base)

        bank = [ctx.enter_context(nc.psum_tensor(f"bank{i}", [P, 512], F32)) for i in range(8)]
        t_bank = [bank[4], bank[5]]
        o_bank, s_bank = bank[6], bank[7]

        w_landed = [sem(f"w_landed{i}") for i in range(4)]
        w_high = sem("w_high")
        w_split = sem("w_split")
        unit_done = sem("unit_done")
        dve_freed = sem("dve_freed")
        act_freed = sem("act_freed")
        st_pe, st_act, st_dve = sem("st_pe"), sem("st_act"), sem("st_dve")
        setup_pool, setup_dve = sem("setup_pool"), sem("setup_dve")
        small_in, cache_in = sem("small_in"), sem("cache_in")
        x_landed = [sem("x_landed0"), sem("x_landed1")]
        x_turned, x_stored = sem("x_turned"), sem("x_stored")
        sq_ready, sq_used, root_ready = sem("sq_ready"), sem("sq_used"), sem("root_ready")
        scaled, high_ready, mean_used = sem("scaled"), sem("high_ready"), sem("mean_used")
        gate_ready, glu_ready, prod_low = sem("gate_ready"), sem("glu_ready"), sem("prod_low")
        prod_high = sem("prod_high")
        v_turned = sem("v_turned")
        chain, act_chain, pool_chain = sem("chain"), sem("act_chain"), sem("pool_chain")
        st_high, st_low = sem("st_high"), sem("st_low")
        scores, shift_ready, exp_done, normed = sem("scores"), sem("shift_ready"), sem("exp_done"), sem("normed")
        turned, turned_high, turned_low = sem("turned"), sem("turned_high"), sem("turned_low")
        pv_done, o_part, o_done = sem("pv_done"), sem("o_part"), sem("o_done")
        out_turned = sem("out_turned")
        out_landed = [sem(f"out_landed{i}") for i in range(2)]
        cache_out = sem("cache_out")
        cache_turned = sem("cache_turned")

        block = ctx.enter_context(nc.Block())
        NST = len(STAGES)

        def parts(b):
            return [(0, TB, False)] + ([(TB, W0, True)] if b == 0 else [])

        def width(b):
            return W0 if b == 0 else TB

        def phys(b, tile):
            cur = b % 2
            return (1 - cur) * NPAIR + tile if tile < NPAIR else cur * NPAIR + tile - NPAIR

        def pairs_before(b):
            return H * sum(n_pairs(i) for i in range(b))

        def tiles_before(b):
            return H * sum(n_key_tiles(i) for i in range(b))

        def key_order(b):
            out = []
            for t in [4, 3, 5, 2, 6, 1, 7, 0]:
                ps = [p for p in range(NPAIR) if (t - p) in band_tiles(b, p)]
                if ps:
                    out.append((t, ps))
            return out

        @block.sync
        def _(sp):
            sp.dma_start(cst[:, :], consts).then_inc(small_in, 16)
            sp.dma_start(bias[:, :, :], rel_near).then_inc(small_in, 16)
            sp.dma_start(probs[:, :, 0:AW], cache_k.rearrange("(t p) n -> p t n", p=P)).then_inc(cache_in, 16)
            sp.dma_start(v[:, NPAIR:2 * NPAIR, :], cache_v.rearrange("(t p) n -> p t n", p=P)).then_inc(cache_in, 16)
            sp.dma_start(nk_sample[0:TB - DEC], cache_k[DEC:TB]).then_inc(cache_out, 16)
            sp.dma_start(nv_sample[0:TB - DEC], cache_v[DEC:TB]).then_inc(cache_out, 16)
            for j in range(4):
                sp.dma_start(w_raw[:, j, :], w_units[j]).then_inc(w_landed[j], 16)
            for b in range(NB):
                with sp.Fori(1 if b == 0 else 0, UNITS // 4) as i:
                    for j in range(4):
                        sp.wait_ge(w_split, i * 4 + (UNITS * b + j - 3))
                        sp.dma_start(w_raw[:, j, :],
                                     w_units[bass.ds(i * 4 + j, 1)].rearrange("a p n -> p (a n)")
                                     ).then_inc(w_landed[j], 16)
            sp.wait_ge(cache_out, 16 * 2)

        @block.gpsimd
        def _(pool):
            pool.memset(tick[:, :], 0.0).then_inc(pool_chain, 1)
            pool.memset(ident[:, :], 0.0).then_inc(pool_chain, 1)
            pool.memset(ones_d[:, :], 1.0 / D).then_inc(pool_chain, 1)
            pool.memset(ones_c[:, :], 1.0 / AW).then_inc(pool_chain, 1)
            pool.memset(q_hi[:, :].bitcast(F32), 0.0).then_inc(pool_chain, 1)
            pool.memset(q_lo[:, :].bitcast(F32), 0.0).then_inc(pool_chain, 1)
            pool.memset(mask_q[:, :].bitcast(F32), 0.0).then_inc(pool_chain, 1)
            pool.memset(mask_k[:, :].bitcast(F32), 0.0).then_inc(pool_chain, 1)
            pool.memset(probs_s[:, :], 0.0).then_inc(pool_chain, 1)
            pool.wait_ge(pool_chain, 9)
            pool.memset(mask_q[0:1, CHUNK:P].bitcast(F32), NEG).then_inc(pool_chain, 1)
            pool.memset(mask_k[0:1, :].bitcast(F32), 1.0).then_inc(pool_chain, 1)
            pool.affine_select(out=ident[:, :], in_=ident[:, :], compare_op=ALU.not_equal, fill=1.0,
                               base=0, pattern=[[-1, P]], channel_multiplier=1).then_inc(pool_chain, 1)
            pool.wait_ge(small_in, 32)
            pool.wait_ge(pool_chain, 12)
            pool.memset(bias[0:CHUNK, :, NEAR - CHUNK:NEAR], NEG).then_inc(setup_pool, 1)

            def split(i, first):
                for j in range(4):
                    pool.wait_ge(w_landed[j], (i + 1) * 16)
                    if not (first and j < 2):
                        pool.wait_ge(unit_done, i * 4 + (j - 1))
                    pool.tensor_tensor(tick[:, 1:2], tick[:, 0:1], tick[:, 0:1], ALU.add)
                    pool.tensor_scalar(w_hi[:, j % 2, :], w_raw[:, j, :], 1.0, 1.0,
                                       ALU.mult, ALU.mult).then_inc(w_high, 1)
                    pool.wait_ge(w_high, i * 4 + (j + 1))
                    pool.tensor_tensor(w_lo[:, j % 2, :], w_raw[:, j, :], w_hi[:, j % 2, :].bitcast(F32),
                                       ALU.subtract).then_inc(w_split, 1)

            split(0, True)
            with pool.Fori(1, NB * UNITS // 4) as i:
                split(i, False)

        @block.tensor
        def _(pe):
            pe.wait_ge(setup_pool, 1)
            stage_no = [0]

            def enter():
                if stage_no[0]:
                    pe.wait_ge(st_act, stage_no[0])
                    pe.wait_ge(st_dve, stage_no[0])

            def leave():
                pe.drain().then_inc(st_pe, 1)
                stage_no[0] += 1

            def linear(b, u0, quads, hi, lo, kt, freed, freed_base):
                with pe.Fori(0, quads) as i:
                    for j in range(4):
                        pe.wait_ge(w_split, i * 4 + (u0 + j + 1))
                        pe.wait_ge(freed, i * 4 + (freed_base + j + 1))
                        for c0, c1, sample in parts(b):
                            out = bank[4 + j][:, 0:DEC] if sample else bank[j][:, :]
                            for k in range(kt):
                                wh = w_hi[:, j % 2, k * P:(k + 1) * P]
                                wl = w_lo[:, j % 2, k * P:(k + 1) * P]
                                pe.matmul(out, wh, hi[:, k, c0:c1], start=(k == 0), stop=False)
                                pe.matmul(out, wh, lo[:, k, c0:c1], start=False, stop=False)
                                last = pe.matmul(out, wl, hi[:, k, c0:c1], start=False, stop=(k == kt - 1))
                        last.then_inc(unit_done, 1)

            def column_sums(b, ones, src, n, n0, out_main, out_sample, sq0):
                for k in range(n):
                    pe.wait_ge(sq_ready, sq0 + k + 1)
                    for c0, c1, sample in parts(b):
                        last = pe.matmul(out_sample if sample else out_main, ones[:, :],
                                         src(k, c0, c1, sample), start=(k == 0), stop=(k == n - 1))
                    last.then_inc(sq_used, 1)

            pe.wait_ge(cache_in, 32)
            for t in range(FT):
                if t >= 2:
                    pe.wait_ge(cache_turned, t - 1)
                for n in range(4):
                    last = pe.transpose(t_bank[t % 2][:, n * P:(n + 1) * P], probs[:, n, t * P:(t + 1) * P],
                                        ident[:, :])
                last.then_inc(x_turned, 1)
            leave()

            x_tiles = 0
            halves = FT
            sq = used = 0
            for b in range(NB):
                enter()
                h0 = halves
                for t in range(n_pairs(b)):
                    rows_in = P if t < NPAIR else DEC
                    pe.wait_ge(x_landed[x_tiles % 2], 16 * (x_tiles // 2 + 1))
                    for half in range(2):
                        if halves - h0 >= 2:
                            pe.wait_ge(x_stored, halves - 1)
                        for n in range(4):
                            k = 4 * half + n
                            last = pe.transpose(t_bank[halves % 2][:, n * P:n * P + rows_in],
                                                x_in[0:rows_in, x_tiles % 2, k * P:(k + 1) * P],
                                                ident[0:rows_in, 0:rows_in])
                        last.then_inc(x_turned, 1)
                        halves += 1
                    x_tiles += 1
                leave()

                def rms_sums():
                    nonlocal sq
                    enter()
                    column_sums(b, ones_d, lambda k, c0, c1, s: tmp[:, k % 2, c0:c1], KD, 0,
                                bank[0][:, :], s_bank[:, 0:DEC], sq)
                    sq += KD
                    leave()

                rms_sums()
                enter()
                linear(b, unit_base(b, "w_in"), 2, a_hi, a_lo, KD, dve_freed, dve_evac_base(b, "w_in"))
                pe.wait_ge(dve_freed, 4 + dve_evac_base(b, "w_in") + 8)
                linear(b, unit_base(b, "w_in") + 8, 3, a_hi, a_lo, KD, act_freed, 12 * b)
                pe.wait_ge(act_freed, 4 + 12 * (b + 1))
                for t in range(FT):
                    if t >= 2:
                        pe.wait_ge(v_turned, FT * b + t - 1)
                    for n in range(NPAIR):
                        last = pe.transpose(t_bank[t % 2][:, n * P:(n + 1) * P], probs[:, t, n * P:(n + 1) * P],
                                            ident[:, :])
                    if b == 0:
                        last = pe.transpose(bank[6 + t % 2][0:DEC, 0:P], probs[:, t, TB:W0], ident[:, :])
                    last.then_inc(x_turned, 1)
                halves += FT
                leave()

                enter()
                order = key_order(b)
                npair, ntile = n_pairs(b), n_key_tiles(b)
                with pe.Fori(0, H // 2) as i:
                    for par in range(2):
                        head = i * 2 + (H * b + par)
                        pair0 = i * (2 * npair) + (pairs_before(b) + par * npair)
                        tile0 = i * (2 * ntile) + (tiles_before(b) + par * ntile)
                        pe.wait_ge(st_high, head + 1)
                        pe.wait_ge(st_low, head + 1)
                        for p in range(npair):
                            pe.wait_ge(exp_done, pair0 + (p + 1))
                            s = 2 * (p % 2)
                            if p == NPAIR:
                                runs = [(s, 0, FAR, TB), (s + 1, 0, P + DEC, TB + FAR)]
                                c0 = TB
                            else:
                                c0 = p * P
                                runs = []
                                for j in band_tiles(b, p):
                                    bk, col = (s, j * P) if j < 3 else (s + 1, (j - 3) * P)
                                    key = phys(b, p + j) * P
                                    if runs and runs[-1][0] == bk and runs[-1][3] + col - runs[-1][1] == key:
                                        runs[-1] = (bk, runs[-1][1], col + P, runs[-1][3])
                                    else:
                                        runs.append((bk, col, col + P, key))
                            for bk, o0, o1, key in runs:
                                masked = p < NPAIR and bk == s and o0 == 0
                                kk = k_st[:, key:key + o1 - o0]
                                pe.matmul(bank[bk][:, o0:o1], q_hi[:, c0:c0 + P], kk, start=True, stop=False)
                                last = pe.matmul(bank[bk][:, o0:o1], q_lo[:, c0:c0 + P], kk, start=False,
                                                 stop=not masked)
                                if masked:
                                    last = pe.matmul(bank[bk][:, 0:CHUNK], mask_q[:, :], mask_k[:, :],
                                                     start=False, stop=True)
                            last.then_inc(scores, 1)
                        pe.wait_ge(o_done, head + 1)
                        pe.wait_ge(normed, pair0 + npair)

                        def turn(n):
                            pe.wait_ge(turned_low, tile0 + (n + 1))
                            tb = t_bank[n % 2]
                            if n < len(order):
                                t, ps = order[n]
                                for p in ps:
                                    last = pe.transpose(tb[:, p * P:(p + 1) * P],
                                                        probs[:, p, (t - p) * P:(t - p + 1) * P], ident[:, :])
                            else:
                                t = n - len(order)
                                w = P if t < 4 else DEC
                                last = pe.transpose(tb[0:w, 0:P], probs_s[:, t * P:t * P + w], ident[:, :])
                            last.then_inc(turned, 1)

                        def weigh(n):
                            pe.wait_ge(turned_low, tile0 + (n + 3))
                            if n < len(order):
                                t, ps = order[n]
                                c0, c1 = ps[0] * P, (ps[-1] + 1) * P
                                vt = v_st[:, phys(b, t), :]
                                out = o_bank[:, c0:c1]
                                pe.matmul(out, vt, pT_hi[:, n % 2, c0:c1], start=(n == 0), stop=False)
                                last = pe.matmul(out, vt, pT_lo[:, n % 2, c0:c1], start=False,
                                                 stop=(n == len(order) - 1))
                            else:
                                t = n - len(order)
                                r = P if t < 4 else DEC
                                vt = v_st[0:r, NPAIR + t, :]
                                out = s_bank[:, 0:DEC]
                                pe.matmul(out, vt, pT_hi[0:r, n % 2, 0:DEC], start=(t == 0), stop=False)
                                last = pe.matmul(out, vt, pT_lo[0:r, n % 2, 0:DEC], start=False, stop=(t == 4))
                            last.then_inc(pv_done, 1)

                        turn(0)
                        for n in range(1, ntile):
                            turn(n)
                            weigh(n - 1)
                        weigh(ntile - 1)
                leave()

                enter()

                def y_cols(c0, c1, s):
                    return (TB + PAST, TB + PAST + DEC) if s else (c0, c1)

                def y_tile(k, c0, c1, s):
                    lo, hi = y_cols(c0, c1, s)
                    return y[:, k, lo:hi]

                for k in range(FT):
                    for c0, c1, s in parts(b):
                        last = pe.matmul(s_bank[:, 0:DEC] if s else bank[0][:, :], ones_c[:, :],
                                         y_tile(k, c0, c1, s), start=(k == 0), stop=(k == FT - 1))
                last.then_inc(mean_used, 1)
                column_sums(b, ones_c, lambda k, c0, c1, s: tmp[:, k % 2, c0:c1], FT, 0,
                            bank[1][:, :], o_bank[:, 0:DEC], sq)
                sq += FT
                if b in (0, NB - 1):
                    lo_, n_tok, n_t = (2 * TB, DEC, 1) if b == 0 else ((b % 2) * TB, P, NPAIR)
                    c0 = 0 if b == 0 else 2
                    for t in range(n_t):
                        if t >= 1:
                            pe.wait_ge(cache_turned, FT + c0 + t)
                        for f in range(FT):
                            last = pe.transpose(t_bank[0][0:n_tok, f * P:(f + 1) * P],
                                                kT[:, f, lo_ + t * P:lo_ + t * P + n_tok], ident[:, :])
                        last.then_inc(x_turned, 1)
                        halves += 1
                    for f in range(FT):
                        last = pe.transpose(t_bank[1][0:PAST, f * P:(f + 1) * P],
                                            (tail_s if b == 0 else tail)[:, f, :], ident[:, :])
                    last.then_inc(x_turned, 1)
                    halves += 1
                leave()

                enter()
                linear(b, unit_base(b, "w_out"), 2, a_hi, a_lo, KD, dve_freed, dve_evac_base(b, "w_out"))
                leave()
                rms_sums()
                for c, nf in enumerate(F_CHUNKS):
                    enter()
                    g = f"gate_up{c}"
                    linear(b, unit_base(b, g), nf // 2, a_hi, a_lo, KD, dve_freed, dve_evac_base(b, g))
                    leave()
                    enter()
                    g = f"down{c}"
                    linear(b, unit_base(b, g), 2, act_hi, act_lo, nf, dve_freed, dve_evac_base(b, g))
                    leave()
                rms_sums()

                enter()
                h0 = halves
                for t in range(n_pairs(b)):
                    n_tok = P if t < NPAIR else DEC
                    for half in range(2):
                        if halves - h0 >= 2:
                            pe.wait_ge(x_stored, halves - 1)
                        for n in range(4):
                            k = 4 * half + n
                            last = pe.transpose(t_bank[halves % 2][0:n_tok, n * P:(n + 1) * P],
                                                x[:, k, t * P:t * P + n_tok], ident[:, :])
                        last.then_inc(x_turned, 1)
                        halves += 1
                leave()

        @block.scalar
        def _(act):
            stage_no = [0]
            act.wait_ge(small_in, 32)
            act.wait_ge(setup_pool, 1)
            act.activation(small[:, 15:16], cst[:, 0:1], ACT.Copy).then_inc(act_freed, 4)
            act.activation(small[:, 14:15], cst[:, 0:1], ACT.Copy).then_inc(exp_done, 2)

            def enter():
                if stage_no[0]:
                    act.wait_ge(st_pe, stage_no[0])
                    act.wait_ge(st_dve, stage_no[0])

            def leave():
                act.drain().then_inc(st_act, 1)
                stage_no[0] += 1

            tiles = [(b, t) for b in range(NB) for t in range(n_pairs(b))]

            def fetch(n):
                if n < len(tiles):
                    b, t = tiles[n]
                    if t < NPAIR:
                        r0 = b * TB + t * P
                        act.dma_start(x_in[:, n % 2, :], x_prompt[r0:r0 + P, :]).then_inc(x_landed[n % 2], 16)
                    else:
                        act.dma_start(x_in[0:DEC, n % 2, :], x_sample).then_inc(x_landed[n % 2], 16)

            fetch(0)
            fetch(1)
            for t in range(FT):
                act.wait_ge(x_turned, t + 1)
                act.activation(kT[:, t, TB:2 * TB], t_bank[t % 2][:, :], ACT.Copy).then_inc(cache_turned, 1)
            leave()

            n_tile = 0
            halves = FT
            stored = 0
            sq = roots = highs = n_scaled = 0
            n_out = [0, 0]
            cached = FT
            n_cache_out = 2
            act.activation(small[:, 13:14], cst[:, 0:1], ACT.Copy).then_inc(x_stored, FT)
            for b in range(NB):
                enter()
                for t in range(n_pairs(b)):
                    n_tok = P if t < NPAIR else DEC
                    for half in range(2):
                        act.wait_ge(x_turned, halves + 1)
                        act.activation(x[:, 4 * half:4 * half + 4, t * P:t * P + n_tok],
                                       t_bank[halves % 2][:, :].rearrange("p (k n) -> p k n", k=4)[:, :, 0:n_tok],
                                       ACT.Copy).then_inc(x_stored, 1)
                        halves += 1
                    fetch(n_tile + 2)
                    n_tile += 1
                leave()

                def squares(src, n):
                    nonlocal sq
                    for k in range(n):
                        if k >= 2:
                            act.wait_ge(sq_used, sq - 1)
                        for c0, c1, s in parts(b):
                            last = act.activation(tmp[:, k % 2, c0:c1], src(k, c0, c1, s), ACT.Square)
                        last.then_inc(sq_ready, 1)
                        sq += 1
                    act.wait_ge(sq_used, sq)

                def root(main, sample, eps):
                    nonlocal roots
                    for c0, c1, s in parts(b):
                        last = act.activation(rstd[:, c0:c1], sample if s else main, ACT.Sqrt, bias=eps)
                    last.then_inc(root_ready, 1)

                def rms(split):
                    nonlocal highs, n_scaled
                    enter()
                    squares(lambda k, c0, c1, s: x[:, k, c0:c1], KD)
                    root(bank[0][:, :], s_bank[:, 0:DEC], eps_rms)
                    if split:
                        for k in range(KD):
                            n_scaled += 1
                            act.wait_ge(scaled, n_scaled)
                            act.activation(a_hi[:, k, 0:width(b)], tmp[:, k % 2, 0:width(b)],
                                           ACT.Copy).then_inc(high_ready, 1)
                            highs += 1
                    leave()

                eps_rms, eps_ln = RMS_EPS, LN_EPS
                rms(True)

                enter()
                u0 = unit_base(b, "w_in")
                for c in range(FT):
                    act.wait_ge(unit_done, u0 + 2 * c + 2)
                    if c >= 2:
                        act.wait_ge(dve_freed, 4 + dve_evac_base(b, "w_in") + 2 * (c - 1))
                    for c0, c1, s in parts(b):
                        j = (2 * c + 1) % 4
                        last = act.activation(tmp[:, c % 2, c0:c1],
                                              bank[4 + j][:, 0:DEC] if s else bank[j][:, :],
                                              ACT.Sigmoid)
                    last.then_inc(gate_ready, 1)
                for n in range(3):
                    for t in range(FT):
                        act.wait_ge(unit_done, u0 + 8 + 4 * n + t + 1)
                        for c0, c1, s in parts(b):
                            src = bank[4 + t][:, 0:DEC] if s else bank[t][:, :]
                            if n == 0:
                                last = act.activation(q[:, t, c0:c1], src, ACT.Copy, scale=Q_SCALE)
                            elif n == 1:
                                k0 = 2 * TB if s else (b % 2) * TB
                                last = act.activation(kT[:, t, k0:k0 + c1 - c0], src, ACT.Copy)
                            else:
                                last = act.activation(probs[:, t, c0:c1], src, ACT.Copy)
                        last.then_inc(act_freed, 1)
                for t in range(FT):
                    act.wait_ge(x_turned, halves + 1)
                    if b == 0:
                        act.activation(v[0:DEC, 2 * NPAIR, t * P:(t + 1) * P],
                                       bank[6 + t % 2][0:DEC, 0:P], ACT.Copy)
                    c = (b % 2) * NPAIR
                    act.activation(v[:, c:c + NPAIR, t * P:(t + 1) * P],
                                   t_bank[t % 2][:, :].rearrange("p (k n) -> p k n", k=4),
                                   ACT.Copy).then_inc(v_turned, 1)
                    halves += 1
                act.activation(small[:, 13:14], cst[:, 0:1], ACT.Copy).then_inc(x_stored, FT)
                leave()

                enter()
                order = key_order(b)
                npair, ntile = n_pairs(b), n_key_tiles(b)
                keys = [(0, 2 * TB)] if b else [(0, TB), (TB, 2 * TB + DEC)]
                with act.Fori(0, H // 2) as i:
                    for par in range(2):
                        r0 = HD * par
                        head = i * 2 + (H * b + par)
                        pair0 = i * (2 * npair) + (pairs_before(b) + par * npair)
                        tile0 = i * (2 * ntile) + (tiles_before(b) + par * ntile)
                        act.wait_ge(o_done, head + 1)
                        qh = q[r0:r0 + HD, bass.ds(i, 1), 0:width(b)]
                        for o in (0, HD):
                            act.activation(q_hi[o:o + HD, 0:width(b)], qh.rearrange("p a n -> p (a n)"), ACT.Copy)
                        kh = kT[r0:r0 + HD, bass.ds(i, 1), keys[0][0]:keys[-1][1]]
                        act.activation(k_st[r0:r0 + HD, keys[0][0]:keys[-1][1]],
                                       kh.rearrange("p a n -> p (a n)"), ACT.Copy)
                        if b == 0:
                            act.activation(v_st[0:DEC, 8, 0:HD], v[0:DEC, 8, bass.ds(i * P + r0, HD)], ACT.Copy)
                        act.activation(v_st[:, 0:8, 0:HD], v[:, 0:8, bass.ds(i * P + r0, HD)],
                                       ACT.Copy).then_inc(st_high, 1)
                        for p in range(npair):
                            act.wait_ge(shift_ready, pair0 + (p + 1))
                            s = 2 * (p % 2)
                            if p == NPAIR:
                                act.activation(probs_s[0:DEC, 0:FAR], bank[s][0:DEC, 0:FAR], ACT.Exp,
                                               bias=small[0:DEC, 2:3], accum_out=small[0:DEC, 4:5])
                                act.activation(probs_s[0:DEC, FAR:544], probs_s[0:DEC, FAR:544], ACT.Exp,
                                               bias=small[0:DEC, 3:4], accum_out=small[0:DEC, 5:6]
                                               ).then_inc(exp_done, 1)
                                continue
                            js = band_tiles(b, p)
                            far0, near0 = js[0] * P, max(js[0] - 3, 0) * P
                            if far0 < FAR:
                                act.activation(probs[:, p, far0:FAR], bank[s][:, far0:FAR], ACT.Exp,
                                               bias=small[:, 2:3], accum_out=small[:, 4:5])
                            act.activation(probs[:, p, FAR + near0:BANDW], probs[:, p, FAR + near0:BANDW],
                                           ACT.Exp, bias=small[:, 3:4], accum_out=small[:, 5:6]
                                           ).then_inc(exp_done, 1)
                        for n in range(ntile):
                            act.wait_ge(turned, tile0 + (n + 1))
                            if n >= 2:
                                act.wait_ge(pv_done, tile0 + (n - 1))
                            if n < len(order):
                                t, ps = order[n]
                                c0, c1 = ps[0] * P, (ps[-1] + 1) * P
                                act.activation(pT_hi[:, n % 2, c0:c1], t_bank[n % 2][:, c0:c1],
                                               ACT.Copy).then_inc(turned_high, 1)
                            else:
                                r = P if n - len(order) < 4 else DEC
                                act.activation(pT_hi[0:r, n % 2, 0:DEC], t_bank[n % 2][0:r, 0:DEC],
                                               ACT.Copy).then_inc(turned_high, 1)
                        act.wait_ge(pv_done, tile0 + ntile)
                        for c0, c1, s in parts(b):
                            last = act.activation(tmp[r0:r0 + HD, 0, c0:c1],
                                                  s_bank[HD:P, 0:DEC] if s else o_bank[HD:P, :], ACT.Copy)
                        last.then_inc(o_part, 1)
                act.wait_ge(o_done, 1 + H * (b + 1))
                act.activation(a_hi[:, 0:FT, 0:width(b)], q[:, :, 0:width(b)], ACT.Copy).then_inc(high_ready, 1)
                highs += 1
                leave()

                enter()

                def y_part(k, c0, c1, s):
                    return y[:, k, TB + PAST:TB + PAST + DEC] if s else y[:, k, c0:c1]

                for k in range(FT):
                    act.wait_ge(glu_ready, (FT + 1) * b + 1 + k)
                    if k >= 2:
                        act.wait_ge(sq_used, sq - 1)
                    for c0, c1, s in parts(b):
                        last = act.activation(tmp[:, k % 2, c0:c1], y_part(k, c0, c1, s), ACT.Square)
                    last.then_inc(sq_ready, 1)
                    sq += 1
                act.wait_ge(sq_used, sq)
                root(bank[1][:, :], o_bank[:, 0:DEC], eps_ln)
                act.wait_ge(glu_ready, (FT + 1) * (b + 1))
                for k in range(FT):
                    if k >= 2:
                        act.wait_ge(prod_low, prod_base(b) + k - 1)
                    for c0, c1, s in parts(b):
                        last = act.activation(tmp[:, k % 2, c0:c1], y_part(k, c0, c1, s), ACT.Silu,
                                              bias=cst[:, C_LNB + k:C_LNB + k + 1],
                                              scale=cst[:, C_LNG + k:C_LNG + k + 1])
                    last.then_inc(act_chain, 1)
                    act.wait_ge(act_chain, FT * b + k + 1)
                    act.activation(a_hi[:, FT + k, 0:width(b)], tmp[:, k % 2, 0:width(b)],
                                   ACT.Copy).then_inc(high_ready, 1)
                    highs += 1
                if b in (0, NB - 1):
                    n_tok, n_t = (DEC, 1) if b == 0 else (P, NPAIR)
                    nk, nv, ncv = (nk_sample, nv_sample, nc_sample) if b == 0 else (nk_prompt, nv_prompt, nc_prompt)
                    r0 = TB - DEC if b == 0 else 0
                    act.wait_ge(prod_low, prod_base(b) + FT)
                    for t in range(n_t):
                        act.wait_ge(x_turned, halves + 1)
                        dst = rows[0:n_tok, t // 2, (t % 2) * AW:(t % 2 + 1) * AW]
                        act.activation(dst, t_bank[0][0:n_tok, :], ACT.Copy).then_inc(cache_turned, 1)
                        cached += 1
                        halves += 1
                        act.wait_ge(cache_turned, cached)
                        act.dma_start(nk[r0 + t * P:r0 + t * P + n_tok, :], dst).then_inc(cache_out, 16)
                    act.wait_ge(x_turned, halves + 1)
                    act.activation(rstd[0:PAST, 0:AW], t_bank[1][0:PAST, :], ACT.Copy).then_inc(cache_turned, 1)
                    cached += 1
                    halves += 1
                    act.wait_ge(cache_turned, cached)
                    act.dma_start(ncv, rstd[0:PAST, 0:AW]).then_inc(cache_out, 16)
                    if b == 0:
                        act.dma_start(nv[r0:r0 + DEC, :], v[0:DEC, 2 * NPAIR, :]).then_inc(cache_out, 16)
                    else:
                        c = (b % 2) * NPAIR
                        act.dma_start(nv.rearrange("(t p) n -> p t n", p=P),
                                      v[:, c:c + NPAIR, :]).then_inc(cache_out, 16)
                    n_cache_out += n_t + 2
                    act.activation(small[:, 13:14], cst[:, 0:1], ACT.Copy).then_inc(x_stored, n_t + 1)
                    act.wait_ge(cache_out, 16 * n_cache_out)
                leave()

                enter()
                leave()
                rms(True)

                for c, nf in enumerate(F_CHUNKS):
                    enter()
                    u0 = unit_base(b, f"gate_up{c}")
                    g0 = ffn_base(b, c)
                    with act.Fori(0, nf // 2) as i:
                        for j in range(2):
                            act.wait_ge(unit_done, i * 4 + (u0 + 2 * j + 1))
                            act.wait_ge(prod_low, i * 2 + (prod_base(b) + FT + sum(F_CHUNKS[:c]) + j + 1 - 2 + 0))
                            for c0, c1, s in parts(b):
                                last = act.activation(tmp[:, j, c0:c1],
                                                      bank[4 + 2 * j][:, 0:DEC] if s
                                                      else bank[2 * j][:, :], ACT.Silu)
                            last.then_inc(gate_ready, 1)
                            act.wait_ge(dve_freed, i * 4 + (4 + dve_evac_base(b, f"gate_up{c}") + 2 * j + 2))
                            act.activation(act_hi[:, bass.ds(i * 2 + j, 1), 0:width(b)].rearrange("p a n -> p (a n)"),
                                           tmp[:, j, 0:width(b)], ACT.Copy).then_inc(prod_high, 1)
                    leave()
                    enter()
                    leave()
                rms(False)

                enter()
                for t in range(n_pairs(b)):
                    n_tok = P if t < NPAIR else DEC
                    if n_out[t % 2]:
                        act.wait_ge(out_landed[t % 2], 16 * n_out[t % 2])
                    for half in range(2):
                        act.wait_ge(x_turned, halves + 1)
                        act.activation(rows[0:n_tok, t % 2, half * 512:(half + 1) * 512],
                                       t_bank[halves % 2][0:n_tok, :], ACT.Copy).then_inc(x_stored, 1)
                        halves += 1
                    act.wait_ge(x_stored, halves)
                    dst = y_prompt[b * TB + t * P:b * TB + (t + 1) * P, :] if t < NPAIR else y_sample
                    act.dma_start(dst, rows[0:n_tok, t % 2, :]).then_inc(out_landed[t % 2], 16)
                    n_out[t % 2] += 1
                for s in range(2):
                    act.wait_ge(out_landed[s], 16 * n_out[s])
                leave()

        @block.vector
        def _(dve):
            stage_no = [0]
            made = [0]

            def link(ins, at=None):
                ins.then_inc(chain, 1)
                made[0] += 1
                dve.wait_ge(chain, made[0] if at is None else at + made[0])

            def enter():
                if stage_no[0]:
                    dve.wait_ge(st_pe, stage_no[0])
                    dve.wait_ge(st_act, stage_no[0])

            def leave():
                dve.drain().then_inc(st_dve, 1)
                stage_no[0] += 1

            dve.memset(tail[:, :, :], 0.0).then_inc(dve_freed, 4)
            dve.memset(small[:, 8:9], 0.0).then_inc(turned_low, 2)
            dve.memset(small[:, 9:10], 0.0).then_inc(o_done, 1)
            dve.wait_ge(small_in, 32)
            leave()
            sq = roots = highs = scaled_n = 0
            for b in range(NB):
                w = width(b)
                enter()
                leave()

                def rms(gain, split):
                    nonlocal roots, highs, scaled_n
                    enter()
                    roots += 1
                    dve.wait_ge(root_ready, roots)
                    link(dve.reciprocal(rstd[:, 0:w], rstd[:, 0:w]))

                    def scale_tile(k):
                        nonlocal scaled_n
                        out = tmp[:, k % 2, 0:w] if split else x[:, k, 0:w]
                        dve.scalar_tensor_tensor(out=out, in0=x[:, k, 0:w], scalar=cst[:, gain + k:gain + k + 1],
                                                 in1=rstd[:, 0:w], op0=ALU.mult, op1=ALU.mult
                                                 ).then_inc(scaled if split else chain, 1)
                        if not split:
                            made[0] += 1

                    if split:
                        scale_tile(0)
                        for k in range(KD):
                            if k + 1 < KD:
                                if k >= 1:
                                    dve.wait_ge(chain, made[0])
                                scale_tile(k + 1)
                            dve.wait_ge(high_ready, highs + 1)
                            highs += 1
                            dve.tensor_tensor(a_lo[:, k, 0:w], tmp[:, k % 2, 0:w], a_hi[:, k, 0:w].bitcast(F32),
                                              ALU.subtract).then_inc(chain, 1)
                            made[0] += 1
                    else:
                        for k in range(KD):
                            scale_tile(k)
                    leave()

                rms(C_GMIX, True)

                enter()
                UWb = UW if b == 0 else PAST + TB
                YWb = YW if b == 0 else TB
                dve.tensor_copy(u[:, :, 0:PAST], tail[:, :, :])
                if b == 0:
                    dve.tensor_copy(u[:, :, PAST + TB:2 * PAST + TB],
                                    cst[:, C_PAST:C_ALL].rearrange("p (c n) -> p c n", c=FT))
                d0 = unit_base(b, "w_in")
                for c in range(FT):
                    dve.wait_ge(gate_ready, gates_base(b) + c + 1)
                    for c0, c1, s in parts(b):
                        j = (2 * c) % 4
                        o = 2 * PAST + TB if s else PAST
                        last = dve.tensor_tensor(u[:, c, o:o + c1 - c0],
                                                 bank[4 + j][:, 0:DEC] if s else bank[j][:, :],
                                                 tmp[:, c % 2, c0:c1], ALU.mult)
                    last.then_inc(dve_freed, 2)
                dve.wait_ge(dve_freed, 4 + dve_evac_base(b, "w_in") + 8)
                dve.tensor_copy(tail[:, :, :], u[:, :, TB:TB + PAST])
                if b == 0:
                    dve.tensor_copy(tail_s[:, :, :], u[:, :, UW - PAST:UW])
                for c in range(FT):
                    last = dve.tensor_scalar(y[:, c, 0:YWb], u[:, c, 0:YWb],
                                             cst[:, C_WDW + c * TAPS:C_WDW + c * TAPS + 1],
                                             cst[:, C_BDW + c:C_BDW + c + 1], ALU.mult, ALU.add)
                    last.then_inc(chain, 1)
                    made[0] += 1
                n0 = made[0]
                with dve.Fori(0, 5) as i:
                    for s in range(6):
                        for c in range(FT):
                            dve.wait_ge(chain, i * 24 + (n0 + s * FT + c - 3))
                            dve.scalar_tensor_tensor(
                                out=y[:, c, 0:YWb], in0=u[:, c, bass.ds(i * 6 + (s + 1), YWb)],
                                scalar=cst[:, bass.ds(i * 6 + (C_WDW + c * TAPS + s + 1), 1)],
                                in1=y[:, c, 0:YWb], op0=ALU.mult, op1=ALU.add).then_inc(chain, 1)
                made[0] += 5 * 24
                leave()

                enter()
                order = key_order(b)
                npair, ntile = n_pairs(b), n_key_tiles(b)
                n_far = sum(band_tiles(b, p)[0] < 3 for p in range(NPAIR)) + (b == 0)
                per_head = 3 * n_far + (npair - n_far) * 2 + n_far + 1 * npair + 0
                per_head = head_links(b)
                n0 = made[0]
                with dve.Fori(0, H // 2) as i:
                    for par in range(2):
                        made[0] = n0 + par * per_head
                        here = i * (2 * per_head)
                        r0, r1 = HD * par, HD * (1 - par)
                        head = i * 2 + (H * b + par)
                        pair0 = i * (2 * npair) + (pairs_before(b) + par * npair)
                        tile0 = i * (2 * ntile) + (tiles_before(b) + par * ntile)
                        dve.wait_ge(st_high, head + 1)
                        qh = q[r0:r0 + HD, bass.ds(i, 1), 0:w].rearrange("p a n -> p (a n)")
                        for o in (0, HD):
                            dve.tensor_tensor(q_lo[o:o + HD, 0:w], qh, q_hi[r0:r0 + HD, 0:w].bitcast(F32),
                                              ALU.subtract)
                        k1 = 2 * TB + DEC if b == 0 else 2 * TB
                        dve.tensor_tensor(k_st[r1:r1 + HD, 0:k1],
                                          kT[r0:r0 + HD, bass.ds(i, 1), 0:k1].rearrange("p a n -> p (a n)"),
                                          k_st[r0:r0 + HD, 0:k1].bitcast(F32), ALU.subtract)
                        if b == 0:
                            dve.tensor_tensor(v_st[0:DEC, 8, HD:P], v[0:DEC, 8, bass.ds(i * P + r0, HD)],
                                              v_st[0:DEC, 8, 0:HD].bitcast(F32), ALU.subtract)
                        dve.tensor_tensor(v_st[:, 0:8, HD:P], v[:, 0:8, bass.ds(i * P + r0, HD)],
                                          v_st[:, 0:8, 0:HD].bitcast(F32), ALU.subtract).then_inc(st_low, 1)

                        def normalize(p):
                            dve.wait_ge(exp_done, pair0 + (2 + p + 1))
                            r = DEC if p == NPAIR else P
                            if p == NPAIR:
                                whole, far = probs_s[0:DEC, :], True
                            else:
                                js = band_tiles(b, p)
                                whole, far = probs[:, p, js[0] * P:BANDW], js[0] < 3
                            if far:
                                link(dve.tensor_tensor(small[0:r, 5:6], small[0:r, 4:5], small[0:r, 5:6], ALU.add),
                                     here)
                            link(dve.reciprocal(small[0:r, 6:7], small[0:r, 5:6]), here)
                            dve.tensor_scalar(whole, whole, small[0:r, 6:7], None, ALU.mult).then_inc(normed, 1)

                        for p in range(npair):
                            dve.wait_ge(scores, pair0 + (p + 1))
                            s = 2 * (p % 2)
                            r = DEC if p == NPAIR else P
                            if p == NPAIR:
                                far0, near0, near1 = 0, 0, 544 - FAR
                                out = probs_s[0:DEC, FAR:544]
                            else:
                                js = band_tiles(b, p)
                                far0, near0, near1 = js[0] * P, max(js[0] - 3, 0) * P, NEAR
                                out = probs[:, p, FAR + near0:BANDW]
                            far = far0 < FAR
                            farb = cst[0:r, bass.ds(i * 2 + (C_FARB + par), 1)]
                            if far:
                                dve.reduce_max(small[0:r, 0:1], bank[s][0:r, far0:FAR], AX_X)
                            hb = bias[0:r, bass.ds(i * 2 + par, 1), near0:near1].rearrange("p a n -> p (a n)")
                            link(dve.tensor_tensor(out, bank[s + 1][0:r, near0:near1], hb, ALU.add), here)
                            link(dve.reduce_max(small[0:r, 1:2], out, AX_X), here)
                            if far:
                                link(dve.tensor_scalar(small[0:r, 1:2], small[0:r, 0:1], farb, small[0:r, 1:2],
                                                       ALU.add, ALU.max), here)
                                dve.tensor_scalar(small[0:r, 2:3], small[0:r, 1:2], -1.0, farb, ALU.mult, ALU.add)
                            dve.tensor_scalar(small[0:r, 3:4], small[0:r, 1:2], -1.0, None,
                                              ALU.mult).then_inc(shift_ready, 1)
                            normalize(p)
                        for n in range(ntile):
                            dve.wait_ge(turned_high, tile0 + (n + 1))
                            if n < len(order):
                                t, ps = order[n]
                                c0, c1, rr = ps[0] * P, (ps[-1] + 1) * P, P
                            else:
                                c0, c1, rr = 0, DEC, (P if n - len(order) < 4 else DEC)
                            dve.tensor_tensor(pT_lo[0:rr, n % 2, c0:c1], t_bank[n % 2][0:rr, c0:c1],
                                              pT_hi[0:rr, n % 2, c0:c1].bitcast(F32),
                                              ALU.subtract).then_inc(turned_low, 1)
                        dve.wait_ge(o_part, head + 1)
                        for c0, c1, s in parts(b):
                            last = dve.tensor_tensor(
                                q[r0:r0 + HD, bass.ds(i, 1), c0:c1].rearrange("p a n -> p (a n)"),
                                s_bank[0:HD, 0:DEC] if s else o_bank[0:HD, :], tmp[r0:r0 + HD, 0, c0:c1], ALU.add)
                        last.then_inc(o_done, 1)
                        assert made[0] == n0 + (par + 1) * per_head, (made[0] - n0 - par * per_head, per_head)
                made[0] = n0 + H * per_head
                dve.wait_ge(high_ready, highs + 1)
                highs += 1
                dve.tensor_tensor(a_lo[:, 0:FT, 0:w], q[:, :, 0:w], a_hi[:, 0:FT, 0:w].bitcast(F32), ALU.subtract)
                leave()

                enter()
                dve.wait_ge(mean_used, b + 1)

                def y_part(k, c0, c1, s):
                    return y[:, k, TB + PAST:TB + PAST + DEC] if s else y[:, k, c0:c1]

                for k in range(FT):
                    for c0, c1, s in parts(b):
                        yp = y_part(k, c0, c1, s)
                        last = dve.tensor_tensor(yp, yp, s_bank[:, 0:DEC] if s else bank[0][:, :], ALU.subtract)
                    last.then_inc(glu_ready, 1)
                roots += 1
                dve.wait_ge(root_ready, roots)
                link(dve.reciprocal(rstd[:, 0:w], rstd[:, 0:w]))
                for k in range(FT):
                    for c0, c1, s in parts(b):
                        yp = y_part(k, c0, c1, s)
                        last = dve.tensor_tensor(yp, yp, rstd[:, c0:c1], ALU.mult)
                last.then_inc(glu_ready, 1)
                for k in range(FT):
                    dve.wait_ge(high_ready, highs + 1)
                    highs += 1
                    dve.tensor_tensor(a_lo[:, FT + k, 0:w], tmp[:, k % 2, 0:w], a_hi[:, FT + k, 0:w].bitcast(F32),
                                      ALU.subtract).then_inc(prod_low, 1)
                leave()

                def add_residual(stage):
                    enter()
                    u0, d0 = unit_base(b, stage), dve_evac_base(b, stage)
                    with dve.Fori(0, 2) as i:
                        for j in range(4):
                            dve.wait_ge(unit_done, i * 4 + (u0 + j + 1))
                            for c0, c1, s in parts(b):
                                xt = x[:, bass.ds(i * 4 + j, 1), c0:c1].rearrange("p a n -> p (a n)")
                                last = dve.tensor_tensor(xt, bank[4 + j][:, 0:DEC] if s else bank[j][:, :],
                                                         xt, ALU.add)
                            last.then_inc(dve_freed, 1)
                    leave()

                add_residual("w_out")
                rms(C_GFFN, True)
                for c, nf in enumerate(F_CHUNKS):
                    enter()
                    u0 = unit_base(b, f"gate_up{c}")
                    g0 = gates_base(b) + FT + sum(F_CHUNKS[:c])
                    h0 = sum(F_CHUNKS) * b + sum(F_CHUNKS[:c])
                    with dve.Fori(0, nf // 2) as i:
                        for j in range(2):
                            dve.wait_ge(gate_ready, i * 2 + (g0 + j + 1))
                            dve.wait_ge(unit_done, i * 4 + (u0 + 2 * j + 2))
                            for c0, c1, s in parts(b):
                                jj = 2 * j + 1
                                last = dve.tensor_tensor(tmp[:, j, c0:c1],
                                                         bank[4 + jj][:, 0:DEC] if s
                                                         else bank[jj][:, :],
                                                         tmp[:, j, c0:c1], ALU.mult)
                            last.then_inc(dve_freed, 2)
                            dve.wait_ge(prod_high, i * 2 + (h0 + j + 1))
                            f = bass.ds(i * 2 + j, 1)
                            dve.tensor_tensor(act_lo[:, f, 0:w].rearrange("p a n -> p (a n)"), tmp[:, j, 0:w],
                                              act_hi[:, f, 0:w].rearrange("p a n -> p (a n)").bitcast(F32),
                                              ALU.subtract).then_inc(prod_low, 1)
                    leave()
                    add_residual(f"down{c}")
                rms(C_GFIN, False)
                enter()
                leave()


def prod_base(b):
    return b * (FT + sum(F_CHUNKS))


def gates_base(b):
    return b * (FT + sum(F_CHUNKS))


def ffn_base(b, c):
    return gates_base(b) + FT + sum(F_CHUNKS[:c])


def head_links(b):
    n = 0
    for p in range(n_pairs(b)):
        far = p == NPAIR or band_tiles(b, p)[0] < 3
        n += 5 if far else 3
    return n


def kernel(**inputs):
    import numpy as np
    import concourse.bacc as bacc
    from concourse.bass_utils import run_bass_kernel_spmd

    nc = bacc.Bacc("TRN2", target_bir_lowering=False, num_devices=1)
    a = {k: np.asarray(v_) for k, v_ in inputs.items()}

    def unit(w, n, k0=0, kt=KD):
        t = w[k0 * P:(k0 + kt) * P, n * P:(n + 1) * P].reshape(kt, P, P).transpose(1, 0, 2).reshape(P, kt * P)
        out = np.zeros((P, D), np.float32)
        out[:, :kt * P] = t
        return out

    w_in, w_out, w_g, w_u, w_d = (a[n][0] for n in ("w_in", "w_out", "w_gate", "w_up", "w_down"))
    units = []
    for c in range(FT):
        units += [unit(w_in, 3 * FT + c), unit(w_in, 4 * FT + c)]
    units += [unit(w_in, n) for n in range(3 * FT)]
    units += [unit(w_out, n) for n in range(KD)]
    f0 = 0
    for nf in F_CHUNKS:
        for f in range(f0, f0 + nf):
            units += [unit(w_g, f), unit(w_u, f)]
        units += [unit(w_d, n, f0, nf) for n in range(KD)]
        f0 += nf

    def columns(vec):
        return vec.reshape(-1, P).T

    table = a["rel_table"][0]
    consts = np.concatenate([
        columns(a["g_mix"][0]), columns(a["g_ffn"][0]), columns(a["g_final"]),
        columns(a["b_dw"][0]), columns(a["ln_g"][0]), columns(a["ln_b"][0]),
        np.broadcast_to(table[:, 2 * CLIP], (P, H)),
        a["w_dw"][0].reshape(TAPS, FT, P).transpose(2, 1, 0).reshape(P, FT * TAPS),
        a["state_conv"][0, 0].reshape(PAST, FT, P).transpose(2, 1, 0).reshape(P, FT * PAST),
    ], axis=1)
    distance = np.arange(P)[:, None] - np.arange(NEAR)[None, :] + P
    rel_near = table[:, np.clip(distance, -CLIP, CLIP) + CLIP].transpose(1, 0, 2)

    arrays = {
        "w_units": np.stack(units),
        "x_prompt": a["x_prompt"][0], "x_sample": a["x_sample"][0],
        "cache_k": a["cache_k"].reshape(TB, AW), "cache_v": a["cache_v"].reshape(TB, AW),
        "consts": consts, "rel_near": rel_near,
    }
    arrays = {k: np.ascontiguousarray(v_) for k, v_ in arrays.items()}
    outs = {"y_prompt": (SEQ, D), "y_sample": (DEC, D), "nk_prompt": (TB, AW), "nv_prompt": (TB, AW),
            "nc_prompt": (PAST, AW), "nk_sample": (TB, AW), "nv_sample": (TB, AW), "nc_sample": (PAST, AW)}
    args = [nc.dram_tensor(k, v_.shape, F32, kind="ExternalInput").ap() for k, v_ in arrays.items()]
    args += [nc.dram_tensor(k, s, F32, kind="ExternalOutput").ap() for k, s in outs.items()]
    build(nc, *args)
    r = run_bass_kernel_spmd(nc, [arrays], core_ids=[0]).results[0]
    return (r["y_prompt"].reshape(1, SEQ, D), r["y_sample"].reshape(1, DEC, D),
            r["nk_prompt"].reshape(1, 1, TB, H, HD), r["nv_prompt"].reshape(1, 1, TB, H, HD),
            r["nc_prompt"].reshape(1, 1, PAST, AW),
            r["nk_sample"].reshape(1, 1, TB, H, HD), r["nv_sample"].reshape(1, 1, TB, H, HD),
            r["nc_sample"].reshape(1, 1, PAST, AW))
```

```python
from contextlib import ExitStack

import concourse.bass as bass
from concourse import mybir

F32 = mybir.dt.float32
F32R = mybir.dt.float32r
ALU = mybir.AluOpType
ACT = mybir.ActivationFunctionType
AX_X = mybir.AxisListType.X

P = 128
D = 1024
KD = D // P
SEQ = 2048
TB = 512
NB = SEQ // TB
DEC = 32
W0 = TB + DEC
H = 8
HD = 64
AW = H * HD
FT = AW // P
CHUNK = 64
NPAIR = TB // P
BANDW = 640
FAR = 384
NEAR = BANDW - FAR
CLIP = 128
TAPS = 31
PAST = TAPS - 1
D_FF = 2816
F_CHUNKS = [8, 8, 6]
RMS_EPS = 1e-6
LN_EPS = 1e-5
NEG = -1e30
Q_SCALE = HD ** -0.5

U_IN, U_OUT = 20, 8
UNITS = U_IN + U_OUT + sum(2 * c + KD for c in F_CHUNKS)

STAGES = ["load", "norm_mix", "w_in", "attend", "conv_norm", "w_out", "norm_ffn"]
for c in range(len(F_CHUNKS)):
    STAGES += [f"gate_up{c}", f"down{c}"]
STAGES += ["norm_final", "store"]

C_GMIX, C_GFFN, C_GFIN = 0, 8, 16
C_BDW, C_LNG, C_LNB = 24, 28, 32
C_FARB = 36
C_WDW = 44
C_PAST = C_WDW + FT * TAPS
C_ALL = C_PAST + FT * PAST


def unit_base(b, stage):
    u = UNITS * b
    if stage == "w_in":
        return u
    if stage == "w_out":
        return u + U_IN
    u += U_IN + U_OUT
    c = int(stage[-1])
    u += sum(2 * f + KD for f in F_CHUNKS[:c])
    return u if stage.startswith("gate_up") else u + 2 * F_CHUNKS[c]


def dve_evac_base(b, stage):
    return unit_base(b, stage) - (U_IN - 8) * (b + (stage != "w_in"))


def band_tiles(b, p):
    return [j for j in range(5) if b > 0 or p + j >= NPAIR]


def n_pairs(b):
    return NPAIR + (b == 0)


def n_key_tiles(b):
    return 9 if b == 0 else 8


def build(nc, w_units, x_prompt, x_sample, cache_k, cache_v, consts, rel_near,
          y_prompt, y_sample, nk_prompt, nv_prompt, nc_prompt, nk_sample, nv_sample, nc_sample):
    ctx = ExitStack()
    with ctx:
        def sb(name, shape, dt=F32):
            return ctx.enter_context(nc.sbuf_tensor(name, shape, dt))

        def sem(name):
            return ctx.enter_context(nc.semaphore(name))

        x = sb("x", [P, KD, W0])
        kT = sb("kT", [P, FT, 2 * TB + DEC])
        v = sb("v", [P, 2 * NPAIR + 1, AW])
        w_raw = sb("w_raw", [P, 4, D])
        w_hi = sb("w_hi", [P, 2, D], F32R)
        w_lo = sb("w_lo", [P, 2, D], F32R)
        bias = sb("bias", [P, H, NEAR])
        cst = sb("cst", [P, C_ALL])
        rstd = sb("rstd", [P, W0])
        tmp = sb("tmp", [P, 2, W0])
        x_in = sb("x_in", [P, 2, D])
        ident = sb("ident", [P, P])
        ones_d = sb("ones_d", [P, P])
        ones_c = sb("ones_c", [P, P])
        mask_q = sb("mask_q", [P, P], F32R)
        mask_k = sb("mask_k", [P, CHUNK], F32R)
        tail = sb("tail", [P, FT, PAST])
        tail_s = sb("tail_s", [P, FT, PAST])
        small = sb("small", [P, 24])
        tick = sb("tick", [P, 2])

        at = [0]

        def reserve(name, n_bytes):
            at[0] = -(-nc.sbuf_base // 32) * 32
            sb(name, [P, n_bytes // 4 + 16])
            return at[0]


        def place(name, shape, dt=F32, start=None):
            if start is not None:
                at[0] = start
            n = 4
            for s in shape[1:]:
                n *= s
            t = nc.alloc_sbuf_tensor_at(name, shape, dt, offset=at[0])
            at[0] += n
            return t

        base = reserve("a_region", 4 * 2 * KD * W0)
        a_hi = place("a_hi", [P, KD, W0], F32R)
        a_lo = place("a_lo", [P, KD, W0], F32R)
        probs1 = place("probs1", [P, NPAIR, BANDW], start=base)
        k_st1 = place("k_st1", [P, 2 * TB + DEC], F32R)
        v_st1 = place("v_st1", [P, 9, P], F32R)
        q_hi1 = place("q_hi1", [P, 640], F32R)
        q_lo1 = place("q_lo1", [P, 640], F32R)
        probs_s1 = place("probs_s1", [P, 544])
        att_bytes = 4 * (FT * W0 + NPAIR * BANDW + 544 + 4 * TB + 2 * 640 + (2 * TB + DEC) + 9 * P)
        act_bytes = 4 * 2 * F_CHUNKS[0] * W0
        base = reserve("att_or_ffn", max(att_bytes, act_bytes))
        q = place("q", [P, FT, W0])
        probs = place("probs", [P, NPAIR, BANDW])
        probs_s = place("probs_s", [P, 544])
        pT_hi = place("pT_hi", [P, 2, TB], F32R)
        pT_lo = place("pT_lo", [P, 2, TB], F32R)
        q_hi = place("q_hi", [P, 640], F32R)
        q_lo = place("q_lo", [P, 640], F32R)
        k_st = place("k_st", [P, 2 * TB + DEC], F32R)
        v_st = place("v_st", [P, 9, P], F32R)
        probs_of, k_of, v_of = [probs, probs1], [k_st, k_st1], [v_st, v_st1]
        probs_s_of = [probs_s, probs_s1]
        q_hi_of, q_lo_of = [q_hi, q_hi1], [q_lo, q_lo1]
        act_hi = place("act_hi", [P, F_CHUNKS[0], W0], F32R, start=base)
        act_lo = place("act_lo", [P, F_CHUNKS[0], W0], F32R)
        UW = PAST + TB + PAST + DEC
        YW = TB + PAST + DEC
        base = reserve("conv_or_rows", 4 * FT * (UW + YW))
        u = place("u", [P, FT, UW])
        y = place("y", [P, FT, YW])
        rows = place("rows", [P, 2, D], start=base)

        bank = [ctx.enter_context(nc.psum_tensor(f"bank{i}", [P, 512], F32)) for i in range(8)]
        t_bank = [bank[4], bank[5]]
        o_bank, s_bank = bank[6], bank[7]

        w_landed = [sem(f"w_landed{i}") for i in range(4)]
        w_high = sem("w_high")
        w_split = sem("w_split")
        unit_done = sem("unit_done")
        dve_freed = sem("dve_freed")
        act_freed = sem("act_freed")
        st_pe, st_act, st_dve = sem("st_pe"), sem("st_act"), sem("st_dve")
        setup_pool, setup_dve = sem("setup_pool"), sem("setup_dve")
        small_in, cache_in = sem("small_in"), sem("cache_in")
        x_landed = [sem("x_landed0"), sem("x_landed1")]
        x_turned, x_stored = sem("x_turned"), sem("x_stored")
        sq_ready, sq_used, root_ready = sem("sq_ready"), sem("sq_used"), sem("root_ready")
        scaled, high_ready, mean_used = sem("scaled"), sem("high_ready"), sem("mean_used")
        gate_ready, glu_ready, prod_low = sem("gate_ready"), sem("glu_ready"), sem("prod_low")
        prod_high = sem("prod_high")
        v_turned = sem("v_turned")
        chain, act_chain, pool_chain = sem("chain"), sem("act_chain"), sem("pool_chain")
        qk_high, qk_low = sem("qk_high"), sem("qk_low")
        v_high, v_low = sem("v_high"), sem("v_low")
        scores, shift_ready, exp_done, normed = sem("scores"), sem("shift_ready"), sem("exp_done"), sem("normed")
        turned, turned_high, turned_low = sem("turned"), sem("turned_high"), sem("turned_low")
        pv_done, o_part, o_done = sem("pv_done"), sem("o_part"), sem("o_done")
        out_turned = sem("out_turned")
        out_landed = [sem(f"out_landed{i}") for i in range(2)]
        cache_out = sem("cache_out")
        cache_turned = sem("cache_turned")

        block = ctx.enter_context(nc.Block())
        NST = len(STAGES)

        def parts(b):
            return [(0, TB, False)] + ([(TB, W0, True)] if b == 0 else [])

        def halves_of(b):
            return [(0, W0 // 2, 0), (W0 // 2, W0, 4)] if b == 0 else [(0, TB, 0)]

        def pieces_of(b):
            if b:
                return [(0, TB, 0, 0, False)]
            m = W0 // 2
            return [(0, m, 0, 0, False), (m, TB, 4, 0, False), (TB, W0, 4, TB - m, True)]

        def width(b):
            return W0 if b == 0 else TB

        def phys(b, tile):
            cur = b % 2
            return (1 - cur) * NPAIR + tile if tile < NPAIR else cur * NPAIR + tile - NPAIR

        def pairs_before(b):
            return H * sum(n_pairs(i) for i in range(b))

        def tiles_before(b):
            return H * sum(n_key_tiles(i) for i in range(b))

        def key_order(b):
            out = []
            for t in [4, 3, 5, 2, 6, 1, 7, 0]:
                ps = [p for p in range(NPAIR) if (t - p) in band_tiles(b, p)]
                if ps:
                    out.append((t, ps))
            return out

        def attend(eng, step):
            step(0, 0, values=False, output=False)
            step(0, 1, output=False)
            with eng.Fori(0, H // 2 - 2) as i:
                step(i, 2)
                step(i, 3)
            step(H // 2 - 2, 2)
            step(H // 2 - 2, 3, last=True)
            step(H // 2 - 1, 2, softmax=False)

        def score_slot(b, h, p):
            return (h * n_pairs(b) + p) % 2

        def key_tiles_at(b, p):
            n, m = n_key_tiles(b), n_pairs(b)
            return range(n * p // m, n * (p + 1) // m)

        @block.sync
        def _(sp):
            sp.dma_start(cst[:, :], consts).then_inc(small_in, 16)
            sp.dma_start(bias[:, :, :], rel_near).then_inc(small_in, 16)
            sp.dma_start(probs[:, :, 0:AW], cache_k.rearrange("(t p) n -> p t n", p=P)).then_inc(cache_in, 16)
            sp.dma_start(v[:, NPAIR:2 * NPAIR, :], cache_v.rearrange("(t p) n -> p t n", p=P)).then_inc(cache_in, 16)
            sp.dma_start(nk_sample[0:TB - DEC], cache_k[DEC:TB]).then_inc(cache_out, 16)
            sp.dma_start(nv_sample[0:TB - DEC], cache_v[DEC:TB]).then_inc(cache_out, 16)
            for j in range(4):
                sp.dma_start(w_raw[:, j, :], w_units[j]).then_inc(w_landed[j], 16)
            for b in range(NB):
                with sp.Fori(1 if b == 0 else 0, UNITS // 4) as i:
                    for j in range(4):
                        sp.wait_ge(w_split, i * 4 + (UNITS * b + j - 3))
                        sp.dma_start(w_raw[:, j, :],
                                     w_units[bass.ds(i * 4 + j, 1)].rearrange("a p n -> p (a n)")
                                     ).then_inc(w_landed[j], 16)
            sp.wait_ge(cache_out, 16 * 2)

        @block.gpsimd
        def _(pool):
            pool.memset(tick[:, :], 0.0).then_inc(pool_chain, 1)
            pool.memset(ident[:, :], 0.0).then_inc(pool_chain, 1)
            pool.memset(ones_d[:, :], 1.0 / D).then_inc(pool_chain, 1)
            pool.memset(ones_c[:, :], 1.0 / AW).then_inc(pool_chain, 1)
            pool.memset(q_hi[:, :].bitcast(F32), 0.0).then_inc(pool_chain, 1)
            pool.memset(q_lo[:, :].bitcast(F32), 0.0).then_inc(pool_chain, 1)
            pool.memset(mask_q[:, :].bitcast(F32), 0.0).then_inc(pool_chain, 1)
            pool.memset(mask_k[:, :].bitcast(F32), 0.0).then_inc(pool_chain, 1)
            pool.memset(probs_s[:, :], 0.0).then_inc(pool_chain, 1)
            pool.wait_ge(pool_chain, 9)
            pool.memset(mask_q[0:1, CHUNK:P].bitcast(F32), NEG).then_inc(pool_chain, 1)
            pool.memset(mask_k[0:1, :].bitcast(F32), 1.0).then_inc(pool_chain, 1)
            pool.affine_select(out=ident[:, :], in_=ident[:, :], compare_op=ALU.not_equal, fill=1.0,
                               base=0, pattern=[[-1, P]], channel_multiplier=1).then_inc(pool_chain, 1)
            pool.wait_ge(small_in, 32)
            pool.wait_ge(pool_chain, 12)
            pool.memset(bias[0:CHUNK, :, NEAR - CHUNK:NEAR], NEG).then_inc(setup_pool, 1)

            def split(i, first):
                for j in range(4):
                    pool.wait_ge(w_landed[j], (i + 1) * 16)
                    if not (first and j < 2):
                        pool.wait_ge(unit_done, i * 4 + (j - 1))
                    pool.tensor_tensor(tick[:, 1:2], tick[:, 0:1], tick[:, 0:1], ALU.add)
                    pool.tensor_scalar(w_hi[:, j % 2, :], w_raw[:, j, :], 1.0, 1.0,
                                       ALU.mult, ALU.mult).then_inc(w_high, 1)
                    pool.wait_ge(w_high, i * 4 + (j + 1))
                    pool.tensor_tensor(w_lo[:, j % 2, :], w_raw[:, j, :], w_hi[:, j % 2, :].bitcast(F32),
                                       ALU.subtract).then_inc(w_split, 1)

            split(0, True)
            with pool.Fori(1, NB * UNITS // 4) as i:
                split(i, False)

        @block.tensor
        def _(pe):
            pe.wait_ge(setup_pool, 1)
            stage_no = [0]

            def enter():
                if stage_no[0]:
                    pe.wait_ge(st_act, stage_no[0])
                    pe.wait_ge(st_dve, stage_no[0])

            def leave():
                pe.drain().then_inc(st_pe, 1)
                stage_no[0] += 1

            def linear(b, u0, quads, hi, lo, kt, freed, freed_base):
                with pe.Fori(0, quads) as i:
                    for j in range(4):
                        pe.wait_ge(w_split, i * 4 + (u0 + j + 1))
                        pe.wait_ge(freed, i * 4 + (freed_base + j + 1))
                        for c0, c1, group in halves_of(b):
                            out = bank[group + j][:, 0:c1 - c0]
                            for k in range(kt):
                                wh = w_hi[:, j % 2, k * P:(k + 1) * P]
                                wl = w_lo[:, j % 2, k * P:(k + 1) * P]
                                pe.matmul(out, wh, hi[:, k, c0:c1], start=(k == 0), stop=False)
                                pe.matmul(out, wh, lo[:, k, c0:c1], start=False, stop=False)
                                last = pe.matmul(out, wl, hi[:, k, c0:c1], start=False, stop=(k == kt - 1))
                        last.then_inc(unit_done, 1)

            def column_sums(b, ones, src, n, n0, out_main, out_sample, sq0):
                for k in range(n):
                    pe.wait_ge(sq_ready, sq0 + k + 1)
                    for c0, c1, sample in parts(b):
                        last = pe.matmul(out_sample if sample else out_main, ones[:, :],
                                         src(k, c0, c1, sample), start=(k == 0), stop=(k == n - 1))
                    last.then_inc(sq_used, 1)

            pe.wait_ge(cache_in, 32)
            for t in range(FT):
                if t >= 2:
                    pe.wait_ge(cache_turned, t - 1)
                for n in range(4):
                    last = pe.transpose(t_bank[t % 2][:, n * P:(n + 1) * P], probs[:, n, t * P:(t + 1) * P],
                                        ident[:, :])
                last.then_inc(x_turned, 1)
            leave()

            x_tiles = 0
            halves = FT
            sq = used = 0
            for b in range(NB):
                enter()
                h0 = halves
                for t in range(n_pairs(b)):
                    rows_in = P if t < NPAIR else DEC
                    pe.wait_ge(x_landed[x_tiles % 2], 16 * (x_tiles // 2 + 1))
                    for half in range(2):
                        if halves - h0 >= 2:
                            pe.wait_ge(x_stored, halves - 1)
                        for n in range(4):
                            k = 4 * half + n
                            last = pe.transpose(t_bank[halves % 2][:, n * P:n * P + rows_in],
                                                x_in[0:rows_in, x_tiles % 2, k * P:(k + 1) * P],
                                                ident[0:rows_in, 0:rows_in])
                        last.then_inc(x_turned, 1)
                        halves += 1
                    x_tiles += 1
                leave()

                def rms_sums():
                    nonlocal sq
                    enter()
                    column_sums(b, ones_d, lambda k, c0, c1, s: tmp[:, k % 2, c0:c1], KD, 0,
                                bank[0][:, :], s_bank[:, 0:DEC], sq)
                    sq += KD
                    leave()

                rms_sums()
                enter()
                linear(b, unit_base(b, "w_in"), 2, a_hi, a_lo, KD, dve_freed, dve_evac_base(b, "w_in"))
                pe.wait_ge(dve_freed, 4 + dve_evac_base(b, "w_in") + 8)
                linear(b, unit_base(b, "w_in") + 8, 3, a_hi, a_lo, KD, act_freed, 12 * b)
                pe.wait_ge(act_freed, 4 + 12 * (b + 1))
                for t in range(FT):
                    if t >= 2:
                        pe.wait_ge(v_turned, FT * b + t - 1)
                    for n in range(NPAIR):
                        last = pe.transpose(t_bank[t % 2][:, n * P:(n + 1) * P], probs[:, t, n * P:(n + 1) * P],
                                            ident[:, :])
                    if b == 0:
                        last = pe.transpose(bank[6 + t % 2][0:DEC, 0:P], probs[:, t, TB:W0], ident[:, :])
                    last.then_inc(x_turned, 1)
                halves += FT
                leave()

                enter()
                order = key_order(b)
                npair, ntile = n_pairs(b), n_key_tiles(b)

                def score(p, h, head, pair0):
                    par = h % 2
                    if p == 0:
                        pe.wait_ge(qk_low, head + 1)
                    pe.wait_ge(exp_done, pair0 + (p + 1))
                    s = 2 * score_slot(b, h, p)
                    if p == NPAIR:
                        runs = [(s, 0, FAR, TB), (s + 1, 0, P + DEC, TB + FAR)]
                        c0 = TB
                    else:
                        c0 = p * P
                        runs = []
                        for j in band_tiles(b, p):
                            bk, col = (s, j * P) if j < 3 else (s + 1, (j - 3) * P)
                            key = phys(b, p + j) * P
                            if runs and runs[-1][0] == bk and runs[-1][3] + col - runs[-1][1] == key:
                                runs[-1] = (bk, runs[-1][1], col + P, runs[-1][3])
                            else:
                                runs.append((bk, col, col + P, key))
                    for bk, o0, o1, key in runs:
                        masked = p < NPAIR and bk == s and o0 == 0
                        kk = k_of[par][:, key:key + o1 - o0]
                        pe.matmul(bank[bk][:, o0:o1], q_hi_of[par][:, c0:c0 + P], kk, start=True, stop=False)
                        last = pe.matmul(bank[bk][:, o0:o1], q_lo_of[par][:, c0:c0 + P], kk, start=False,
                                         stop=not masked)
                        if masked:
                            last = pe.matmul(bank[bk][:, 0:CHUNK], mask_q[:, :], mask_k[:, :],
                                             start=False, stop=True)
                    last.then_inc(scores, 1)

                def turn(n, par, tile0):
                    pe.wait_ge(turned_low, tile0 + (n + 1))
                    tb = t_bank[n % 2]
                    if n < len(order):
                        t, ps = order[n]
                        for p in ps:
                            last = pe.transpose(tb[:, p * P:(p + 1) * P],
                                                probs_of[par][:, p, (t - p) * P:(t - p + 1) * P], ident[:, :])
                    else:
                        t = n - len(order)
                        w = P if t < 4 else DEC
                        last = pe.transpose(tb[0:w, 0:P], probs_s_of[par][:, t * P:t * P + w], ident[:, :])
                    last.then_inc(turned, 1)

                def weigh(n, par, tile0):
                    pe.wait_ge(turned_low, tile0 + (n + 3))
                    if n < len(order):
                        t, ps = order[n]
                        c0, c1 = ps[0] * P, (ps[-1] + 1) * P
                        vt = v_of[par][:, phys(b, t), :]
                        out = o_bank[:, c0:c1]
                        pe.matmul(out, vt, pT_hi[:, n % 2, c0:c1], start=(n == 0), stop=False)
                        last = pe.matmul(out, vt, pT_lo[:, n % 2, c0:c1], start=False, stop=(n == len(order) - 1))
                    else:
                        t = n - len(order)
                        r = P if t < 4 else DEC
                        vt = v_of[par][0:r, NPAIR + t, :]
                        out = s_bank[:, 0:DEC]
                        pe.matmul(out, vt, pT_hi[0:r, n % 2, 0:DEC], start=(t == 0), stop=False)
                        last = pe.matmul(out, vt, pT_lo[0:r, n % 2, 0:DEC], start=False, stop=(t == 4))
                    last.then_inc(pv_done, 1)

                def step(i, h, softmax=True, values=True, output=True, last=False):
                    head = i * 2 + (H * b + h)
                    pair0 = i * (2 * npair) + (pairs_before(b) + h * npair)
                    tile0 = i * (2 * ntile) + (tiles_before(b) + (h - 1) * ntile)
                    before = (h - 1) % 2
                    if softmax and not values:
                        score(0, h, head, pair0)
                    weighed = 0
                    if values:
                        pe.wait_ge(normed, pair0)
                    for p in range(npair):
                        if values:
                            for n in key_tiles_at(b, p):
                                turn(n, before, tile0)
                                if p and weighed < n - 1:
                                    if weighed == 0:
                                        pe.wait_ge(v_low, head)
                                        pe.wait_ge(o_done, head)
                                    weigh(weighed, before, tile0)
                                    weighed += 1
                        if softmax and p + 1 < npair:
                            score(p + 1, h, head, pair0)
                        elif softmax and not last:
                            score(0, h + 1, head + 1, pair0 + npair)
                    if values:
                        while weighed < ntile:
                            weigh(weighed, before, tile0)
                            weighed += 1

                attend(pe, step)
                leave()

                enter()

                def y_cols(c0, c1, s):
                    return (TB + PAST, TB + PAST + DEC) if s else (c0, c1)

                def y_tile(k, c0, c1, s):
                    lo, hi = y_cols(c0, c1, s)
                    return y[:, k, lo:hi]

                for k in range(FT):
                    for c0, c1, s in parts(b):
                        last = pe.matmul(s_bank[:, 0:DEC] if s else bank[0][:, :], ones_c[:, :],
                                         y_tile(k, c0, c1, s), start=(k == 0), stop=(k == FT - 1))
                last.then_inc(mean_used, 1)
                column_sums(b, ones_c, lambda k, c0, c1, s: tmp[:, k % 2, c0:c1], FT, 0,
                            bank[1][:, :], o_bank[:, 0:DEC], sq)
                sq += FT
                if b in (0, NB - 1):
                    lo_, n_tok, n_t = (2 * TB, DEC, 1) if b == 0 else ((b % 2) * TB, P, NPAIR)
                    c0 = 0 if b == 0 else 2
                    for t in range(n_t):
                        if t >= 1:
                            pe.wait_ge(cache_turned, FT + c0 + t)
                        for f in range(FT):
                            last = pe.transpose(t_bank[0][0:n_tok, f * P:(f + 1) * P],
                                                kT[:, f, lo_ + t * P:lo_ + t * P + n_tok], ident[:, :])
                        last.then_inc(x_turned, 1)
                        halves += 1
                    for f in range(FT):
                        last = pe.transpose(t_bank[1][0:PAST, f * P:(f + 1) * P],
                                            (tail_s if b == 0 else tail)[:, f, :], ident[:, :])
                    last.then_inc(x_turned, 1)
                    halves += 1
                leave()

                enter()
                linear(b, unit_base(b, "w_out"), 2, a_hi, a_lo, KD, dve_freed, dve_evac_base(b, "w_out"))
                leave()
                rms_sums()
                for c, nf in enumerate(F_CHUNKS):
                    enter()
                    g = f"gate_up{c}"
                    linear(b, unit_base(b, g), nf // 2, a_hi, a_lo, KD, dve_freed, dve_evac_base(b, g))
                    leave()
                    enter()
                    g = f"down{c}"
                    linear(b, unit_base(b, g), 2, act_hi, act_lo, nf, dve_freed, dve_evac_base(b, g))
                    leave()
                rms_sums()

                enter()
                h0 = halves
                for t in range(n_pairs(b)):
                    n_tok = P if t < NPAIR else DEC
                    for half in range(2):
                        if halves - h0 >= 2:
                            pe.wait_ge(x_stored, halves - 1)
                        for n in range(4):
                            k = 4 * half + n
                            last = pe.transpose(t_bank[halves % 2][0:n_tok, n * P:(n + 1) * P],
                                                x[:, k, t * P:t * P + n_tok], ident[:, :])
                        last.then_inc(x_turned, 1)
                        halves += 1
                leave()

        @block.scalar
        def _(act):
            stage_no = [0]
            act.wait_ge(small_in, 32)
            act.wait_ge(setup_pool, 1)
            act.activation(small[:, 23:24], cst[:, 0:1], ACT.Copy).then_inc(act_freed, 4)
            act.activation(small[:, 22:23], cst[:, 0:1], ACT.Copy).then_inc(exp_done, 2)

            def enter():
                if stage_no[0]:
                    act.wait_ge(st_pe, stage_no[0])
                    act.wait_ge(st_dve, stage_no[0])

            def leave():
                act.drain().then_inc(st_act, 1)
                stage_no[0] += 1

            tiles = [(b, t) for b in range(NB) for t in range(n_pairs(b))]

            def fetch(n):
                if n < len(tiles):
                    b, t = tiles[n]
                    if t < NPAIR:
                        r0 = b * TB + t * P
                        act.dma_start(x_in[:, n % 2, :], x_prompt[r0:r0 + P, :]).then_inc(x_landed[n % 2], 16)
                    else:
                        act.dma_start(x_in[0:DEC, n % 2, :], x_sample).then_inc(x_landed[n % 2], 16)

            fetch(0)
            fetch(1)
            for t in range(FT):
                act.wait_ge(x_turned, t + 1)
                act.activation(kT[:, t, TB:2 * TB], t_bank[t % 2][:, :], ACT.Copy).then_inc(cache_turned, 1)
            leave()

            n_tile = 0
            halves = FT
            stored = 0
            sq = roots = highs = n_scaled = 0
            n_out = [0, 0]
            cached = FT
            n_cache_out = 2
            act.activation(small[:, 21:22], cst[:, 0:1], ACT.Copy).then_inc(x_stored, FT)
            for b in range(NB):
                enter()
                for t in range(n_pairs(b)):
                    n_tok = P if t < NPAIR else DEC
                    for half in range(2):
                        act.wait_ge(x_turned, halves + 1)
                        act.activation(x[:, 4 * half:4 * half + 4, t * P:t * P + n_tok],
                                       t_bank[halves % 2][:, :].rearrange("p (k n) -> p k n", k=4)[:, :, 0:n_tok],
                                       ACT.Copy).then_inc(x_stored, 1)
                        halves += 1
                    fetch(n_tile + 2)
                    n_tile += 1
                leave()

                def squares(src, n):
                    nonlocal sq
                    for k in range(n):
                        if k >= 2:
                            act.wait_ge(sq_used, sq - 1)
                        for c0, c1, s in parts(b):
                            last = act.activation(tmp[:, k % 2, c0:c1], src(k, c0, c1, s), ACT.Square)
                        last.then_inc(sq_ready, 1)
                        sq += 1
                    act.wait_ge(sq_used, sq)

                def root(main, sample, eps):
                    nonlocal roots
                    for c0, c1, s in parts(b):
                        last = act.activation(rstd[:, c0:c1], sample if s else main, ACT.Sqrt, bias=eps)
                    last.then_inc(root_ready, 1)

                def rms(split):
                    nonlocal highs, n_scaled
                    enter()
                    squares(lambda k, c0, c1, s: x[:, k, c0:c1], KD)
                    root(bank[0][:, :], s_bank[:, 0:DEC], eps_rms)
                    if split:
                        for k in range(KD):
                            n_scaled += 1
                            act.wait_ge(scaled, n_scaled)
                            act.activation(a_hi[:, k, 0:width(b)], tmp[:, k % 2, 0:width(b)],
                                           ACT.Copy).then_inc(high_ready, 1)
                            highs += 1
                    leave()

                eps_rms, eps_ln = RMS_EPS, LN_EPS
                rms(True)

                enter()
                u0 = unit_base(b, "w_in")
                for c in range(FT):
                    act.wait_ge(unit_done, u0 + 2 * c + 2)
                    if c >= 2:
                        act.wait_ge(dve_freed, 4 + dve_evac_base(b, "w_in") + 2 * (c - 1))
                    for c0, c1, group in halves_of(b):
                        last = act.activation(tmp[:, c % 2, c0:c1],
                                              bank[group + (2 * c + 1) % 4][:, 0:c1 - c0], ACT.Sigmoid)
                    last.then_inc(gate_ready, 1)
                for n in range(3):
                    for t in range(FT):
                        act.wait_ge(unit_done, u0 + 8 + 4 * n + t + 1)
                        for c0, c1, group, off, s in pieces_of(b):
                            src = bank[group + t][:, off:off + c1 - c0]
                            if n == 0:
                                last = act.activation(q[:, t, c0:c1], src, ACT.Copy, scale=Q_SCALE)
                            elif n == 1:
                                k0 = 2 * TB if s else (b % 2) * TB + c0
                                last = act.activation(kT[:, t, k0:k0 + c1 - c0], src, ACT.Copy)
                            else:
                                last = act.activation(probs[:, t, c0:c1], src, ACT.Copy)
                        last.then_inc(act_freed, 1)
                for t in range(FT):
                    act.wait_ge(x_turned, halves + 1)
                    if b == 0:
                        act.activation(v[0:DEC, 2 * NPAIR, t * P:(t + 1) * P],
                                       bank[6 + t % 2][0:DEC, 0:P], ACT.Copy)
                    c = (b % 2) * NPAIR
                    act.activation(v[:, c:c + NPAIR, t * P:(t + 1) * P],
                                   t_bank[t % 2][:, :].rearrange("p (k n) -> p k n", k=4),
                                   ACT.Copy).then_inc(v_turned, 1)
                    halves += 1
                act.activation(small[:, 21:22], cst[:, 0:1], ACT.Copy).then_inc(x_stored, FT)
                leave()

                enter()
                order = key_order(b)
                npair, ntile = n_pairs(b), n_key_tiles(b)
                k1 = 2 * TB + DEC if b == 0 else 2 * TB

                def qk_operands(i, h):
                    r0, par = HD * (h % 2), h % 2
                    hp = bass.ds(i + h // 2, 1) if not isinstance(i, int) else slice(i + h // 2, i + h // 2 + 1)
                    qh = q[r0:r0 + HD, hp, 0:width(b)].rearrange("p a n -> p (a n)")
                    for o in (0, HD):
                        act.activation(q_hi_of[par][o:o + HD, 0:width(b)], qh, ACT.Copy)
                    act.activation(k_of[par][r0:r0 + HD, 0:k1], kT[r0:r0 + HD, hp, 0:k1].rearrange("p a n -> p (a n)"),
                                   ACT.Copy).then_inc(qk_high, 1)

                def v_operand(i, h):
                    par = h % 2
                    cols = bass.ds(i * P + h * HD, HD)
                    if b == 0:
                        act.activation(v_of[par][0:DEC, 8, 0:HD], v[0:DEC, 8, cols], ACT.Copy)
                    act.activation(v_of[par][:, 0:8, 0:HD], v[:, 0:8, cols], ACT.Copy).then_inc(v_high, 1)

                def exponentials(p, h, pair0):
                    act.wait_ge(shift_ready, pair0 + (p + 1))
                    slot, par = score_slot(b, h, p), h % 2
                    s, m = 2 * slot, 8 * slot
                    if p == NPAIR:
                        act.activation(probs_s_of[par][0:DEC, 0:FAR], bank[s][0:DEC, 0:FAR], ACT.Exp,
                                       bias=small[0:DEC, m + 2:m + 3], accum_out=small[0:DEC, m + 4:m + 5])
                        act.activation(probs_s_of[par][0:DEC, FAR:544], probs_s_of[par][0:DEC, FAR:544], ACT.Exp,
                                       bias=small[0:DEC, m + 3:m + 4], accum_out=small[0:DEC, m + 5:m + 6]
                                       ).then_inc(exp_done, 1)
                        return
                    js = band_tiles(b, p)
                    far0, near0 = js[0] * P, max(js[0] - 3, 0) * P
                    if far0 < FAR:
                        act.activation(probs_of[par][:, p, far0:FAR], bank[s][:, far0:FAR], ACT.Exp,
                                       bias=small[:, m + 2:m + 3], accum_out=small[:, m + 4:m + 5])
                    near = probs_of[par][:, p, FAR + near0:BANDW]
                    act.activation(near, near, ACT.Exp, bias=small[:, m + 3:m + 4],
                                   accum_out=small[:, m + 5:m + 6]).then_inc(exp_done, 1)

                def high_tile(n, tile0):
                    act.wait_ge(turned, tile0 + (n + 1))
                    if n >= 2:
                        act.wait_ge(pv_done, tile0 + (n - 1))
                    if n < len(order):
                        t, ps = order[n]
                        c0, c1, r = ps[0] * P, (ps[-1] + 1) * P, P
                    else:
                        c0, c1, r = 0, DEC, (P if n - len(order) < 4 else DEC)
                    act.activation(pT_hi[0:r, n % 2, c0:c1], t_bank[n % 2][0:r, c0:c1],
                                   ACT.Copy).then_inc(turned_high, 1)

                def take_output(i, h):
                    r0 = HD * (h % 2)
                    act.wait_ge(pv_done, i * (2 * ntile) + (tiles_before(b) + (h + 1) * ntile))
                    for c0, c1, s in parts(b):
                        last = act.activation(tmp[r0:r0 + HD, 0, c0:c1],
                                              s_bank[HD:P, 0:DEC] if s else o_bank[HD:P, :], ACT.Copy)
                    last.then_inc(o_part, 1)

                def step(i, h, softmax=True, values=True, output=True, last=False):
                    pair0 = i * (2 * npair) + (pairs_before(b) + h * npair)
                    tile0 = i * (2 * ntile) + (tiles_before(b) + (h - 1) * ntile)
                    for p in range(npair):
                        if values:
                            for n in key_tiles_at(b, p):
                                high_tile(n, tile0)
                        if p == 0 and output:
                            take_output(i, h - 2)
                        if softmax:
                            exponentials(p, h, pair0)
                            if p == 0:
                                v_operand(i, h)
                            if p == 1 and not last:
                                qk_operands(i, h + 1)

                qk_operands(0, 0)
                attend(act, step)
                take_output(H // 2 - 1, 1)
                act.wait_ge(o_done, 1 + H * (b + 1))
                act.activation(a_hi[:, 0:FT, 0:width(b)], q[:, :, 0:width(b)], ACT.Copy).then_inc(high_ready, 1)
                highs += 1
                leave()

                enter()

                def y_part(k, c0, c1, s):
                    return y[:, k, TB + PAST:TB + PAST + DEC] if s else y[:, k, c0:c1]

                for k in range(FT):
                    act.wait_ge(glu_ready, (FT + 1) * b + 1 + k)
                    if k >= 2:
                        act.wait_ge(sq_used, sq - 1)
                    for c0, c1, s in parts(b):
                        last = act.activation(tmp[:, k % 2, c0:c1], y_part(k, c0, c1, s), ACT.Square)
                    last.then_inc(sq_ready, 1)
                    sq += 1
                act.wait_ge(sq_used, sq)
                root(bank[1][:, :], o_bank[:, 0:DEC], eps_ln)
                act.wait_ge(glu_ready, (FT + 1) * (b + 1))
                for k in range(FT):
                    if k >= 2:
                        act.wait_ge(prod_low, prod_base(b) + k - 1)
                    for c0, c1, s in parts(b):
                        last = act.activation(tmp[:, k % 2, c0:c1], y_part(k, c0, c1, s), ACT.Silu,
                                              bias=cst[:, C_LNB + k:C_LNB + k + 1],
                                              scale=cst[:, C_LNG + k:C_LNG + k + 1])
                    last.then_inc(act_chain, 1)
                    act.wait_ge(act_chain, FT * b + k + 1)
                    act.activation(a_hi[:, FT + k, 0:width(b)], tmp[:, k % 2, 0:width(b)],
                                   ACT.Copy).then_inc(high_ready, 1)
                    highs += 1
                if b in (0, NB - 1):
                    n_tok, n_t = (DEC, 1) if b == 0 else (P, NPAIR)
                    nk, nv, ncv = (nk_sample, nv_sample, nc_sample) if b == 0 else (nk_prompt, nv_prompt, nc_prompt)
                    r0 = TB - DEC if b == 0 else 0
                    act.wait_ge(prod_low, prod_base(b) + FT)
                    for t in range(n_t):
                        act.wait_ge(x_turned, halves + 1)
                        dst = rows[0:n_tok, t // 2, (t % 2) * AW:(t % 2 + 1) * AW]
                        act.activation(dst, t_bank[0][0:n_tok, :], ACT.Copy).then_inc(cache_turned, 1)
                        cached += 1
                        halves += 1
                        act.wait_ge(cache_turned, cached)
                        act.dma_start(nk[r0 + t * P:r0 + t * P + n_tok, :], dst).then_inc(cache_out, 16)
                    act.wait_ge(x_turned, halves + 1)
                    act.activation(rstd[0:PAST, 0:AW], t_bank[1][0:PAST, :], ACT.Copy).then_inc(cache_turned, 1)
                    cached += 1
                    halves += 1
                    act.wait_ge(cache_turned, cached)
                    act.dma_start(ncv, rstd[0:PAST, 0:AW]).then_inc(cache_out, 16)
                    if b == 0:
                        act.dma_start(nv[r0:r0 + DEC, :], v[0:DEC, 2 * NPAIR, :]).then_inc(cache_out, 16)
                    else:
                        c = (b % 2) * NPAIR
                        act.dma_start(nv.rearrange("(t p) n -> p t n", p=P),
                                      v[:, c:c + NPAIR, :]).then_inc(cache_out, 16)
                    n_cache_out += n_t + 2
                    act.activation(small[:, 21:22], cst[:, 0:1], ACT.Copy).then_inc(x_stored, n_t + 1)
                    act.wait_ge(cache_out, 16 * n_cache_out)
                leave()

                enter()
                leave()
                rms(True)

                for c, nf in enumerate(F_CHUNKS):
                    enter()
                    u0 = unit_base(b, f"gate_up{c}")
                    g0 = ffn_base(b, c)
                    with act.Fori(0, nf // 2) as i:
                        for j in range(2):
                            act.wait_ge(unit_done, i * 4 + (u0 + 2 * j + 1))
                            act.wait_ge(prod_low, i * 2 + (prod_base(b) + FT + sum(F_CHUNKS[:c]) + j + 1 - 2 + 0))
                            for c0, c1, group in halves_of(b):
                                last = act.activation(tmp[:, j, c0:c1], bank[group + 2 * j][:, 0:c1 - c0],
                                                      ACT.Silu)
                            last.then_inc(gate_ready, 1)
                            act.wait_ge(dve_freed, i * 4 + (4 + dve_evac_base(b, f"gate_up{c}") + 2 * j + 2))
                            act.activation(act_hi[:, bass.ds(i * 2 + j, 1), 0:width(b)].rearrange("p a n -> p (a n)"),
                                           tmp[:, j, 0:width(b)], ACT.Copy).then_inc(prod_high, 1)
                    leave()
                    enter()
                    leave()
                rms(False)

                enter()
                for t in range(n_pairs(b)):
                    n_tok = P if t < NPAIR else DEC
                    if n_out[t % 2]:
                        act.wait_ge(out_landed[t % 2], 16 * n_out[t % 2])
                    for half in range(2):
                        act.wait_ge(x_turned, halves + 1)
                        act.activation(rows[0:n_tok, t % 2, half * 512:(half + 1) * 512],
                                       t_bank[halves % 2][0:n_tok, :], ACT.Copy).then_inc(x_stored, 1)
                        halves += 1
                    act.wait_ge(x_stored, halves)
                    dst = y_prompt[b * TB + t * P:b * TB + (t + 1) * P, :] if t < NPAIR else y_sample
                    act.dma_start(dst, rows[0:n_tok, t % 2, :]).then_inc(out_landed[t % 2], 16)
                    n_out[t % 2] += 1
                for s in range(2):
                    act.wait_ge(out_landed[s], 16 * n_out[s])
                leave()

        @block.vector
        def _(dve):
            stage_no = [0]
            made = [0]

            def link(ins, at=None, lag=0):
                ins.then_inc(chain, 1)
                made[0] += 1
                dve.wait_ge(chain, made[0] - lag if at is None else at + (made[0] - lag))

            def enter():
                if stage_no[0]:
                    dve.wait_ge(st_pe, stage_no[0])
                    dve.wait_ge(st_act, stage_no[0])

            def leave():
                dve.drain().then_inc(st_dve, 1)
                stage_no[0] += 1

            dve.memset(tail[:, :, :], 0.0).then_inc(dve_freed, 4)
            dve.memset(small[:, 20:21], 0.0).then_inc(turned_low, 2)
            dve.memset(small[:, 19:20], 0.0).then_inc(o_done, 1)
            dve.wait_ge(small_in, 32)
            leave()
            sq = roots = highs = scaled_n = 0
            for b in range(NB):
                w = width(b)
                enter()
                leave()

                def rms(gain, split):
                    nonlocal roots, highs, scaled_n
                    enter()
                    roots += 1
                    dve.wait_ge(root_ready, roots)
                    link(dve.reciprocal(rstd[:, 0:w], rstd[:, 0:w]))

                    def scale_tile(k):
                        nonlocal scaled_n
                        out = tmp[:, k % 2, 0:w] if split else x[:, k, 0:w]
                        dve.scalar_tensor_tensor(out=out, in0=x[:, k, 0:w], scalar=cst[:, gain + k:gain + k + 1],
                                                 in1=rstd[:, 0:w], op0=ALU.mult, op1=ALU.mult
                                                 ).then_inc(scaled if split else chain, 1)
                        if not split:
                            made[0] += 1

                    if split:
                        scale_tile(0)
                        for k in range(KD):
                            if k + 1 < KD:
                                if k >= 1:
                                    dve.wait_ge(chain, made[0])
                                scale_tile(k + 1)
                            dve.wait_ge(high_ready, highs + 1)
                            highs += 1
                            dve.tensor_tensor(a_lo[:, k, 0:w], tmp[:, k % 2, 0:w], a_hi[:, k, 0:w].bitcast(F32),
                                              ALU.subtract).then_inc(chain, 1)
                            made[0] += 1
                    else:
                        for k in range(KD):
                            scale_tile(k)
                    leave()

                rms(C_GMIX, True)

                enter()
                UWb = UW if b == 0 else PAST + TB
                YWb = YW if b == 0 else TB
                dve.tensor_copy(u[:, :, 0:PAST], tail[:, :, :])
                if b == 0:
                    dve.tensor_copy(u[:, :, PAST + TB:2 * PAST + TB],
                                    cst[:, C_PAST:C_ALL].rearrange("p (c n) -> p c n", c=FT))
                d0 = unit_base(b, "w_in")
                for c in range(FT):
                    dve.wait_ge(gate_ready, gates_base(b) + c + 1)
                    for c0, c1, group, off, s in pieces_of(b):
                        o = c0 + (2 * PAST if s else PAST)
                        last = dve.tensor_tensor(u[:, c, o:o + c1 - c0],
                                                 bank[group + (2 * c) % 4][:, off:off + c1 - c0],
                                                 tmp[:, c % 2, c0:c1], ALU.mult)
                    last.then_inc(dve_freed, 2)
                dve.wait_ge(dve_freed, 4 + dve_evac_base(b, "w_in") + 8)
                dve.tensor_copy(tail[:, :, :], u[:, :, TB:TB + PAST])
                if b == 0:
                    dve.tensor_copy(tail_s[:, :, :], u[:, :, UW - PAST:UW])
                for c in range(FT):
                    last = dve.tensor_scalar(y[:, c, 0:YWb], u[:, c, 0:YWb],
                                             cst[:, C_WDW + c * TAPS:C_WDW + c * TAPS + 1],
                                             cst[:, C_BDW + c:C_BDW + c + 1], ALU.mult, ALU.add)
                    last.then_inc(chain, 1)
                    made[0] += 1
                n0 = made[0]
                with dve.Fori(0, 5) as i:
                    for s in range(6):
                        for c in range(FT):
                            dve.wait_ge(chain, i * 24 + (n0 + s * FT + c - 3))
                            dve.scalar_tensor_tensor(
                                out=y[:, c, 0:YWb], in0=u[:, c, bass.ds(i * 6 + (s + 1), YWb)],
                                scalar=cst[:, bass.ds(i * 6 + (C_WDW + c * TAPS + s + 1), 1)],
                                in1=y[:, c, 0:YWb], op0=ALU.mult, op1=ALU.add).then_inc(chain, 1)
                made[0] += 5 * 24
                leave()

                enter()
                order = key_order(b)
                npair, ntile = n_pairs(b), n_key_tiles(b)
                per_head = head_links(b)
                k1 = 2 * TB + DEC if b == 0 else 2 * TB
                n0 = made[0]
                if b == 0:
                    for t in (q_hi1, q_lo1):
                        dve.memset(t[:, W0:640].bitcast(F32), 0.0)
                    dve.memset(probs_s1[:, :], 0.0).then_inc(chain, 1)
                    made[0] += 1
                    n0 = made[0]
                    dve.wait_ge(chain, n0)

                def qk_operands(i, h):
                    r0, r1, par = HD * (h % 2), HD * (1 - h % 2), h % 2
                    hp = bass.ds(i + h // 2, 1) if not isinstance(i, int) else slice(i + h // 2, i + h // 2 + 1)
                    dve.wait_ge(qk_high, i * 2 + (H * b + h + 1))
                    qh = q[r0:r0 + HD, hp, 0:w].rearrange("p a n -> p (a n)")
                    for o in (0, HD):
                        dve.tensor_tensor(q_lo_of[par][o:o + HD, 0:w], qh,
                                          q_hi_of[par][r0:r0 + HD, 0:w].bitcast(F32), ALU.subtract)
                    dve.tensor_tensor(k_of[par][r1:r1 + HD, 0:k1],
                                      kT[r0:r0 + HD, hp, 0:k1].rearrange("p a n -> p (a n)"),
                                      k_of[par][r0:r0 + HD, 0:k1].bitcast(F32), ALU.subtract).then_inc(qk_low, 1)

                def v_operand(i, h):
                    vs = v_of[h % 2]
                    cols = bass.ds(i * P + h * HD, HD)
                    dve.wait_ge(v_high, i * 2 + (H * b + h + 1))
                    if b == 0:
                        dve.tensor_tensor(vs[0:DEC, 8, HD:P], v[0:DEC, 8, cols], vs[0:DEC, 8, 0:HD].bitcast(F32),
                                          ALU.subtract)
                    dve.tensor_tensor(vs[:, 0:8, HD:P], v[:, 0:8, cols], vs[:, 0:8, 0:HD].bitcast(F32),
                                      ALU.subtract).then_inc(v_low, 1)

                def shifts(i, p, h, pair0, here):
                    dve.wait_ge(scores, pair0 + (p + 1))
                    s, m = 2 * score_slot(b, h, p), 8 * score_slot(b, h, p)
                    r = DEC if p == NPAIR else P
                    if p == NPAIR:
                        far0, near0, near1 = 0, 0, 544 - FAR
                        out = probs_s_of[h % 2][0:DEC, FAR:544]
                    else:
                        js = band_tiles(b, p)
                        far0, near0, near1 = js[0] * P, max(js[0] - 3, 0) * P, NEAR
                        out = probs_of[h % 2][:, p, FAR + near0:BANDW]
                    far_max, top = small[0:r, m:m + 1], small[0:r, m + 1:m + 2]
                    farb = cst[0:r, bass.ds(i * 2 + (C_FARB + h), 1)]
                    hb = bias[0:r, bass.ds(i * 2 + h, 1), near0:near1].rearrange("p a n -> p (a n)")
                    if far0 < FAR:
                        link(dve.tensor_tensor(out, bank[s + 1][0:r, near0:near1], hb, ALU.add), here, 1)
                        link(dve.reduce_max(far_max, bank[s][0:r, far0:FAR], AX_X), here, 1)
                        link(dve.reduce_max(top, out, AX_X), here)
                        link(dve.tensor_scalar(top, far_max, farb, top, ALU.add, ALU.max), here)
                        dve.tensor_scalar(small[0:r, m + 2:m + 3], top, -1.0, farb, ALU.mult, ALU.add)
                    else:
                        link(dve.tensor_tensor(out, bank[s + 1][0:r, near0:near1], hb, ALU.add), here)
                        link(dve.reduce_max(top, out, AX_X), here)
                    dve.tensor_scalar(small[0:r, m + 3:m + 4], top, -1.0, None, ALU.mult).then_inc(shift_ready, 1)

                def normalize(p, h, pair0, here):
                    dve.wait_ge(exp_done, pair0 + (2 + p + 1))
                    m = 8 * score_slot(b, h, p)
                    if p == NPAIR:
                        r, whole, far = DEC, probs_s_of[h % 2][0:DEC, :], True
                    else:
                        js = band_tiles(b, p)
                        r, whole, far = P, probs_of[h % 2][:, p, js[0] * P:BANDW], js[0] < 3
                    total, inverse = small[0:r, m + 5:m + 6], small[0:r, m + 6:m + 7]
                    if far:
                        link(dve.tensor_tensor(total, small[0:r, m + 4:m + 5], total, ALU.add), here)
                    link(dve.reciprocal(inverse, total), here)
                    dve.tensor_scalar(whole, whole, inverse, None, ALU.mult).then_inc(normed, 1)

                def low_tile(n, tile0):
                    dve.wait_ge(turned_high, tile0 + (n + 1))
                    if n < len(order):
                        t, ps = order[n]
                        c0, c1, rr = ps[0] * P, (ps[-1] + 1) * P, P
                    else:
                        c0, c1, rr = 0, DEC, (P if n - len(order) < 4 else DEC)
                    dve.tensor_tensor(pT_lo[0:rr, n % 2, c0:c1], t_bank[n % 2][0:rr, c0:c1],
                                      pT_hi[0:rr, n % 2, c0:c1].bitcast(F32), ALU.subtract).then_inc(turned_low, 1)

                def take_output(i, h):
                    r0 = HD * (h % 2)
                    hp = bass.ds(i + h // 2, 1) if not isinstance(i, int) else slice(i + h // 2, i + h // 2 + 1)
                    dve.wait_ge(o_part, i * 2 + (H * b + h + 1))
                    for c0, c1, s in parts(b):
                        last = dve.tensor_tensor(
                            q[r0:r0 + HD, hp, c0:c1].rearrange("p a n -> p (a n)"),
                            s_bank[0:HD, 0:DEC] if s else o_bank[0:HD, :], tmp[r0:r0 + HD, 0, c0:c1], ALU.add)
                    last.then_inc(o_done, 1)

                def step(i, h, softmax=True, values=True, output=True, last=False):
                    made[0] = n0 + h * per_head
                    here = i * (2 * per_head)
                    pair0 = i * (2 * npair) + (pairs_before(b) + h * npair)
                    tile0 = i * (2 * ntile) + (tiles_before(b) + (h - 1) * ntile)
                    for p in range(npair):
                        if softmax:
                            shifts(i, p, h, pair0, here)
                        if values:
                            for n in key_tiles_at(b, p):
                                low_tile(n, tile0)
                        if p == 0 and output:
                            take_output(i, h - 2)
                        if softmax:
                            if p:
                                normalize(p - 1, h, pair0, here)
                            if p == 1:
                                v_operand(i, h)
                            if p == 2 and not last:
                                qk_operands(i, h + 1)
                    if softmax:
                        normalize(npair - 1, h, pair0, here)
                        assert made[0] == n0 + (h + 1) * per_head, (made[0] - n0 - h * per_head, per_head)

                qk_operands(0, 0)
                attend(dve, step)
                take_output(H // 2 - 1, 1)
                made[0] = n0 + H * per_head
                dve.wait_ge(high_ready, highs + 1)
                highs += 1
                dve.tensor_tensor(a_lo[:, 0:FT, 0:w], q[:, :, 0:w], a_hi[:, 0:FT, 0:w].bitcast(F32), ALU.subtract)
                leave()

                enter()
                dve.wait_ge(mean_used, b + 1)

                def y_part(k, c0, c1, s):
                    return y[:, k, TB + PAST:TB + PAST + DEC] if s else y[:, k, c0:c1]

                for k in range(FT):
                    for c0, c1, s in parts(b):
                        yp = y_part(k, c0, c1, s)
                        last = dve.tensor_tensor(yp, yp, s_bank[:, 0:DEC] if s else bank[0][:, :], ALU.subtract)
                    last.then_inc(glu_ready, 1)
                roots += 1
                dve.wait_ge(root_ready, roots)
                link(dve.reciprocal(rstd[:, 0:w], rstd[:, 0:w]))
                for k in range(FT):
                    for c0, c1, s in parts(b):
                        yp = y_part(k, c0, c1, s)
                        last = dve.tensor_tensor(yp, yp, rstd[:, c0:c1], ALU.mult)
                last.then_inc(glu_ready, 1)
                for k in range(FT):
                    dve.wait_ge(high_ready, highs + 1)
                    highs += 1
                    dve.tensor_tensor(a_lo[:, FT + k, 0:w], tmp[:, k % 2, 0:w], a_hi[:, FT + k, 0:w].bitcast(F32),
                                      ALU.subtract).then_inc(prod_low, 1)
                leave()

                def add_residual(stage):
                    enter()
                    u0, d0 = unit_base(b, stage), dve_evac_base(b, stage)
                    with dve.Fori(0, 2) as i:
                        for j in range(4):
                            dve.wait_ge(unit_done, i * 4 + (u0 + j + 1))
                            for c0, c1, group in halves_of(b):
                                xt = x[:, bass.ds(i * 4 + j, 1), c0:c1].rearrange("p a n -> p (a n)")
                                last = dve.tensor_tensor(xt, bank[group + j][:, 0:c1 - c0], xt, ALU.add)
                            last.then_inc(dve_freed, 1)
                    leave()

                add_residual("w_out")
                rms(C_GFFN, True)
                for c, nf in enumerate(F_CHUNKS):
                    enter()
                    u0 = unit_base(b, f"gate_up{c}")
                    g0 = gates_base(b) + FT + sum(F_CHUNKS[:c])
                    h0 = sum(F_CHUNKS) * b + sum(F_CHUNKS[:c])
                    with dve.Fori(0, nf // 2) as i:
                        for j in range(2):
                            dve.wait_ge(gate_ready, i * 2 + (g0 + j + 1))
                            dve.wait_ge(unit_done, i * 4 + (u0 + 2 * j + 2))
                            for c0, c1, group in halves_of(b):
                                last = dve.tensor_tensor(tmp[:, j, c0:c1], bank[group + 2 * j + 1][:, 0:c1 - c0],
                                                         tmp[:, j, c0:c1], ALU.mult)
                            last.then_inc(dve_freed, 2)
                            dve.wait_ge(prod_high, i * 2 + (h0 + j + 1))
                            f = bass.ds(i * 2 + j, 1)
                            dve.tensor_tensor(act_lo[:, f, 0:w].rearrange("p a n -> p (a n)"), tmp[:, j, 0:w],
                                              act_hi[:, f, 0:w].rearrange("p a n -> p (a n)").bitcast(F32),
                                              ALU.subtract).then_inc(prod_low, 1)
                    leave()
                    add_residual(f"down{c}")
                rms(C_GFIN, False)
                enter()
                leave()


def prod_base(b):
    return b * (FT + sum(F_CHUNKS))


def gates_base(b):
    return b * (FT + sum(F_CHUNKS))


def ffn_base(b, c):
    return gates_base(b) + FT + sum(F_CHUNKS[:c])


def head_links(b):
    n = 0
    for p in range(n_pairs(b)):
        far = p == NPAIR or band_tiles(b, p)[0] < 3
        n += 6 if far else 3
    return n


def kernel(**inputs):
    import numpy as np
    import concourse.bacc as bacc
    from concourse.bass_utils import run_bass_kernel_spmd

    nc = bacc.Bacc("TRN2", target_bir_lowering=False, num_devices=1)
    a = {k: np.asarray(v_) for k, v_ in inputs.items()}

    def unit(w, n, k0=0, kt=KD):
        t = w[k0 * P:(k0 + kt) * P, n * P:(n + 1) * P].reshape(kt, P, P).transpose(1, 0, 2).reshape(P, kt * P)
        out = np.zeros((P, D), np.float32)
        out[:, :kt * P] = t
        return out

    w_in, w_out, w_g, w_u, w_d = (a[n][0] for n in ("w_in", "w_out", "w_gate", "w_up", "w_down"))
    units = []
    for c in range(FT):
        units += [unit(w_in, 3 * FT + c), unit(w_in, 4 * FT + c)]
    units += [unit(w_in, n) for n in range(3 * FT)]
    units += [unit(w_out, n) for n in range(KD)]
    f0 = 0
    for nf in F_CHUNKS:
        for f in range(f0, f0 + nf):
            units += [unit(w_g, f), unit(w_u, f)]
        units += [unit(w_d, n, f0, nf) for n in range(KD)]
        f0 += nf

    def columns(vec):
        return vec.reshape(-1, P).T

    table = a["rel_table"][0]
    consts = np.concatenate([
        columns(a["g_mix"][0]), columns(a["g_ffn"][0]), columns(a["g_final"]),
        columns(a["b_dw"][0]), columns(a["ln_g"][0]), columns(a["ln_b"][0]),
        np.broadcast_to(table[:, 2 * CLIP], (P, H)),
        a["w_dw"][0].reshape(TAPS, FT, P).transpose(2, 1, 0).reshape(P, FT * TAPS),
        a["state_conv"][0, 0].reshape(PAST, FT, P).transpose(2, 1, 0).reshape(P, FT * PAST),
    ], axis=1)
    distance = np.arange(P)[:, None] - np.arange(NEAR)[None, :] + P
    rel_near = table[:, np.clip(distance, -CLIP, CLIP) + CLIP].transpose(1, 0, 2)

    arrays = {
        "w_units": np.stack(units),
        "x_prompt": a["x_prompt"][0], "x_sample": a["x_sample"][0],
        "cache_k": a["cache_k"].reshape(TB, AW), "cache_v": a["cache_v"].reshape(TB, AW),
        "consts": consts, "rel_near": rel_near,
    }
    arrays = {k: np.ascontiguousarray(v_) for k, v_ in arrays.items()}
    outs = {"y_prompt": (SEQ, D), "y_sample": (DEC, D), "nk_prompt": (TB, AW), "nv_prompt": (TB, AW),
            "nc_prompt": (PAST, AW), "nk_sample": (TB, AW), "nv_sample": (TB, AW), "nc_sample": (PAST, AW)}
    args = [nc.dram_tensor(k, v_.shape, F32, kind="ExternalInput").ap() for k, v_ in arrays.items()]
    args += [nc.dram_tensor(k, s, F32, kind="ExternalOutput").ap() for k, s in outs.items()]
    build(nc, *args)
    r = run_bass_kernel_spmd(nc, [arrays], core_ids=[0]).results[0]
    return (r["y_prompt"].reshape(1, SEQ, D), r["y_sample"].reshape(1, DEC, D),
            r["nk_prompt"].reshape(1, 1, TB, H, HD), r["nv_prompt"].reshape(1, 1, TB, H, HD),
            r["nc_prompt"].reshape(1, 1, PAST, AW),
            r["nk_sample"].reshape(1, 1, TB, H, HD), r["nv_sample"].reshape(1, 1, TB, H, HD),
            r["nc_sample"].reshape(1, 1, PAST, AW))
```

```python
from contextlib import ExitStack

import concourse.bass as bass
from concourse import mybir

F32 = mybir.dt.float32
F32R = mybir.dt.float32r
ALU = mybir.AluOpType
ACT = mybir.ActivationFunctionType
AX_X = mybir.AxisListType.X

P = 128
D = 1024
KD = D // P
SEQ = 2048
TB = 512
NB = SEQ // TB
DEC = 32
W0 = TB + DEC
H = 8
HD = 64
AW = H * HD
FT = AW // P
CHUNK = 64
NPAIR = TB // P
BANDW = 640
FAR = 384
NEAR = BANDW - FAR
CLIP = 128
TAPS = 31
PAST = TAPS - 1
D_FF = 2816
F_CHUNKS = [8, 8, 6]
assert sum(F_CHUNKS) * P == D_FF
RMS_EPS = 1e-6
LN_EPS = 1e-5
NEG = -1e30
Q_SCALE = HD ** -0.5

U_IN, U_OUT = 20, 8
UNITS = U_IN + U_OUT + sum(2 * c + KD for c in F_CHUNKS)

C_GMIX, C_GFFN, C_GFIN = 0, 8, 16
C_BDW, C_LNG, C_LNB = 24, 28, 32
C_FARB = 36
C_WDW = 44
C_PAST = C_WDW + FT * TAPS
C_ALL = C_PAST + FT * PAST


def unit_base(b, stage):
    u = UNITS * b
    if stage == "w_in":
        return u
    if stage == "w_out":
        return u + U_IN
    u += U_IN + U_OUT
    c = int(stage[-1])
    u += sum(2 * f + KD for f in F_CHUNKS[:c])
    return u if stage.startswith("gate_up") else u + 2 * F_CHUNKS[c]


def dve_evac_base(b, stage):
    return unit_base(b, stage) - (U_IN - 8) * (b + (stage != "w_in"))


def band_tiles(b, p):
    return [j for j in range(5) if b > 0 or p + j >= NPAIR]


def n_pairs(b):
    return NPAIR + (b == 0)


def build(nc, w_units, x_prompt, x_sample, cache_k, cache_v, consts, rel_near,
          y_prompt, y_sample, nk_prompt, nv_prompt, nc_prompt, nk_sample, nv_sample, nc_sample):
    ctx = ExitStack()
    with ctx:
        def sb(name, shape, dt=F32):
            return ctx.enter_context(nc.sbuf_tensor(name, shape, dt))

        def sem(name):
            return ctx.enter_context(nc.semaphore(name))

        x = sb("x", [P, KD, W0])
        kT = sb("kT", [P, FT, 2 * TB + DEC])
        v = sb("v", [P, 2 * NPAIR + 1, AW])
        w_raw = sb("w_raw", [P, 4, D])
        w_hi = sb("w_hi", [P, 2, D], F32R)
        w_lo = sb("w_lo", [P, 2, D], F32R)
        bias = sb("bias", [P, H, NEAR])
        cst = sb("cst", [P, C_ALL])
        rstd = sb("rstd", [P, W0])
        tmp = sb("tmp", [P, 2, W0])
        x_in = sb("x_in", [P, 2, D])
        ident = sb("ident", [P, P])
        ones_d = sb("ones_d", [P, P])
        ones_c = sb("ones_c", [P, P])
        mask_q = sb("mask_q", [P, P], F32R)
        mask_k = sb("mask_k", [P, CHUNK], F32R)
        tail = sb("tail", [P, FT, PAST])
        tail_s = sb("tail_s", [P, FT, PAST])
        credit = sb("credit", [P, 8])
        rms_in = sb("rms_in", [P, NPAIR + 1])
        rms_out = sb("rms_out", [P, 2 * (NPAIR + 1)])
        shift = sb("shift", [P, NPAIR + 1, 4])
        sums = sb("sums", [P, 2, 2, NPAIR + 1])
        inverse = sb("inverse", [P, NPAIR + 1])
        tick = sb("tick", [P, 2])

        at = [0]

        def reserve(name, n_bytes):
            at[0] = -(-nc.sbuf_base // 32) * 32
            sb(name, [P, n_bytes // 4 + 16])
            return at[0]

        def place(name, shape, dt=F32, start=None):
            if start is not None:
                at[0] = start
            n = 4
            for s in shape[1:]:
                n *= s
            t = nc.alloc_sbuf_tensor_at(name, shape, dt, offset=at[0])
            at[0] += n
            return t

        base = reserve("a_region", 4 * 2 * KD * W0)
        a_hi = place("a_hi", [P, KD, W0], F32R)
        a_lo = place("a_lo", [P, KD, W0], F32R)
        pT = place("pT", [P, 2, BANDW], start=base)
        k_st1 = place("k_st1", [P, 2 * TB + DEC], F32R)
        q_hi1 = place("q_hi1", [P, 640], F32R)
        q_lo1 = place("q_lo1", [P, 640], F32R)
        att_bytes = 4 * (FT * W0 + (NPAIR + 1) * (AW + BANDW) + 2 * 640 + 2 * TB + DEC)
        ffn_bytes = 4 * 2 * KD * W0
        base = reserve("att_or_ffn", max(att_bytes, ffn_bytes + 4 * 2 * D))
        q = place("q", [P, FT, W0])
        o_tok = place("o_tok", [P, NPAIR + 1, AW])
        probs = place("probs", [P, NPAIR + 1, BANDW])
        q_hi = place("q_hi", [P, 640], F32R)
        q_lo = place("q_lo", [P, 640], F32R)
        k_st = place("k_st", [P, 2 * TB + DEC], F32R)
        k_of, q_hi_of, q_lo_of = [k_st, k_st1], [q_hi, q_hi1], [q_lo, q_lo1]
        f_hi = place("f_hi", [P, KD, W0], F32R, start=base)
        f_lo = place("f_lo", [P, KD, W0], F32R)
        x_in2 = place("x_in2", [P, 2, D])
        UW = PAST + TB + PAST + DEC
        YW = TB + PAST + DEC
        base = reserve("conv_or_rows", 4 * FT * (UW + YW))
        u = place("u", [P, FT, UW])
        y = place("y", [P, FT, YW])
        rows = place("rows", [P, NPAIR, D], start=base)

        bank = [ctx.enter_context(nc.psum_tensor(f"bank{i}", [P, 512], F32)) for i in range(8)]
        t_bank = [bank[4], bank[5]]
        far_bank, near_bank = bank[4], bank[5]
        o_bank = [bank[6], bank[7]]
        io_bank = [[bank[4], bank[5]], [bank[6], bank[7]]]

        w_landed = [sem(f"w_landed{i}") for i in range(4)]
        w_high = sem("w_high")
        w_split = sem("w_split")
        unit_done = sem("unit_done")
        dve_freed = sem("dve_freed")
        act_freed = sem("act_freed")
        st_pe, st_act, st_dve = sem("st_pe"), sem("st_act"), sem("st_dve")
        setup_pool = sem("setup_pool")
        small_in, bias_in = sem("small_in"), sem("bias_in")
        cache_k_in, cache_v_in = sem("cache_k_in"), sem("cache_v_in")
        x_landed = [sem(f"x_landed{i}") for i in range(NPAIR + 1)]
        io_turned, io_act, io_dve = sem("io_turned"), sem("io_act"), sem("io_dve")
        col_root, diag_ready, rstd_spread = sem("col_root"), sem("diag_ready"), sem("rstd_spread")
        sq_ready, sq_used, summed, root_ready = sem("sq_ready"), sem("sq_used"), sem("summed"), sem("root_ready")
        scaled, high_ready, a_low = sem("scaled"), sem("high_ready"), sem("a_low")
        y_sum, mean_ready, centred = sem("y_sum"), sem("mean_ready"), sem("centred")
        conv_rstd, y_scaled = sem("conv_rstd"), sem("y_scaled")
        gate_scaled, gate_ready = sem("gate_scaled"), sem("gate_ready")
        prod_high, prod_low = sem("prod_high"), sem("prod_low")
        v_turned_pe, v_turned = sem("v_turned_pe"), sem("v_turned")
        x_gained, out_summed, out_root, out_rstd = sem("x_gained"), sem("out_summed"), sem("out_root"), sem("out_rstd")
        chain, act_chain, pool_chain = sem("chain"), sem("act_chain"), sem("pool_chain")
        qk_high, qk_low = sem("qk_high"), sem("qk_low")
        scores, shift_ready = sem("scores"), sem("shift_ready")
        far_exp, exp_done = sem("far_exp"), sem("exp_done")
        far_turned, near_turned = sem("far_turned"), sem("near_turned")
        far_copied, near_copied = sem("far_copied"), sem("near_copied")
        pv_done, totals, o_done, o_turned = sem("pv_done"), sem("totals"), sem("o_done"), sem("o_turned")
        out_landed = [sem(f"out_landed{i}") for i in range(NPAIR + 1)]
        cache_out = sem("cache_out")
        cache_turned_pe, cache_turned = sem("cache_turned_pe"), sem("cache_turned")

        block = ctx.enter_context(nc.Block())

        def parts(b):
            return [(0, TB, False)] + ([(TB, W0, True)] if b == 0 else [])

        def halves_of(b):
            return [(0, W0 // 2, 0), (W0 // 2, W0, 4)] if b == 0 else [(0, TB, 0)]

        def pieces_of(b):
            if b:
                return [(0, TB, 0, 0, False)]
            m = W0 // 2
            return [(0, m, 0, 0, False), (m, TB, 4, 0, False), (TB, W0, 4, TB - m, True)]

        def y_part(k, c0, c1, s):
            return y[:, k, TB + PAST:TB + PAST + DEC] if s else y[:, k, c0:c1]

        def width(b):
            return W0 if b == 0 else TB

        def phys(b, tile):
            cur = b % 2
            return (1 - cur) * NPAIR + tile if tile < NPAIR else cur * NPAIR + tile - NPAIR

        def pairs_before(b):
            return H * sum(n_pairs(i) for i in range(b))

        def far_pairs(b):
            return [p for p in range(n_pairs(b)) if p == NPAIR or band_tiles(b, p)[0] < 3]

        def fars_before(b, h, p):
            return (H * sum(len(far_pairs(i)) for i in range(b)) + h * len(far_pairs(b))
                    + sum(f < p for f in far_pairs(b)))

        def input_tile(t):
            return x_in[:, t, :] if t < 2 else x_in2[:, t - 2, :] if t < NPAIR else rows[0:DEC, 0, :]

        def tokens(t):
            return P if t < NPAIR else DEC

        def squares_base(b, part):
            return 20 * b + {"conv": 0, "w_out": FT, "down": FT + KD}[part]

        def low_base(b, part):
            return 3 * KD * b + {"w_in": 0, "w_out": KD, "gate_up": 2 * KD}[part]

        def prod_base(b, c):
            return sum(F_CHUNKS) * b + sum(F_CHUNKS[:c])

        def gate_base(b, c):
            return (FT + sum(F_CHUNKS)) * b + FT + sum(F_CHUNKS[:c])

        CUT = (0, NB - 1)

        def attend(eng, step):
            step(0, 0, first=True)
            step(0, 1, second=True)
            with eng.Fori(0, H // 2 - 2) as i:
                step(i, 2)
                step(i, 3)
            step(H // 2 - 2, 2, ending=True)
            step(H // 2 - 2, 3, ending=True, last=True)

        def pair_slot(b, h, p):
            return (h * n_pairs(b) + p) % 2

        def head_tile(i, h):
            return slice(i + h // 2, i + h // 2 + 1) if isinstance(i, int) else bass.ds(i + h // 2, 1)

        def tile_parts(b, p):
            if p == NPAIR:
                return [(0, P), (1, P), (2, P)], [(3, P), (4, DEC)]
            js = band_tiles(b, p)
            return [(j, P) for j in js if j < 3], [(j, P) for j in js if j >= 3]

        @block.sync
        def _(sp):
            sp.dma_start(cst[:, :], consts).then_inc(small_in, 16)
            for j in range(4):
                sp.dma_start(w_raw[:, j, :], w_units[j]).then_inc(w_landed[j], 16)
            sp.dma_start(o_tok[:, 0:NPAIR, :], cache_k.rearrange("(t p) n -> p t n", p=P)).then_inc(cache_k_in, 16)
            sp.dma_start(bias[:, :, :], rel_near).then_inc(bias_in, 16)
            sp.dma_start(v[:, NPAIR:2 * NPAIR, :], cache_v.rearrange("(t p) n -> p t n", p=P)).then_inc(cache_v_in, 16)
            sp.dma_start(nk_sample[0:TB - DEC], cache_k[DEC:TB]).then_inc(cache_out, 16)
            sp.dma_start(nv_sample[0:TB - DEC], cache_v[DEC:TB]).then_inc(cache_out, 16)
            for b in range(NB):
                with sp.Fori(1 if b == 0 else 0, UNITS // 4) as i:
                    for j in range(4):
                        sp.wait_ge(w_split, i * 4 + (UNITS * b + j - 3))
                        sp.dma_start(w_raw[:, j, :],
                                     w_units[bass.ds(i * 4 + j, 1)].rearrange("a p n -> p (a n)")
                                     ).then_inc(w_landed[j], 16)
            sp.wait_ge(cache_out, 16 * 2)

        @block.gpsimd
        def _(pool):
            pool.memset(tick[:, :], 0.0).then_inc(pool_chain, 1)
            pool.memset(ident[:, :], 0.0).then_inc(pool_chain, 1)
            pool.memset(ones_d[:, :], 1.0 / D).then_inc(pool_chain, 1)
            pool.memset(ones_c[:, :], 1.0 / AW).then_inc(pool_chain, 1)
            pool.memset(mask_q[:, :].bitcast(F32), 0.0).then_inc(pool_chain, 1)
            pool.memset(mask_k[:, :].bitcast(F32), 0.0).then_inc(pool_chain, 1)
            pool.memset(probs[:, NPAIR, :], 0.0).then_inc(pool_chain, 1)
            pool.wait_ge(pool_chain, 7)
            pool.memset(mask_q[0:1, CHUNK:P].bitcast(F32), NEG).then_inc(pool_chain, 1)
            pool.memset(mask_k[0:1, :].bitcast(F32), 1.0).then_inc(pool_chain, 1)
            pool.affine_select(out=ident[:, :], in_=ident[:, :], compare_op=ALU.not_equal, fill=1.0,
                               base=0, pattern=[[-1, P]], channel_multiplier=1).then_inc(setup_pool, 1)

            def split(i, js=range(4), first=False):
                for j in js:
                    pool.wait_ge(w_landed[j], (i + 1) * 16)
                    if not (first and j < 2):
                        pool.wait_ge(unit_done, i * 4 + (j - 1))
                    pool.tensor_tensor(tick[:, 1:2], tick[:, 0:1], tick[:, 0:1], ALU.add)
                    pool.tensor_scalar(w_hi[:, j % 2, :], w_raw[:, j, :], 1.0, 1.0,
                                       ALU.mult, ALU.mult).then_inc(w_high, 1)
                    pool.wait_ge(w_high, i * 4 + (j + 1))
                    pool.tensor_tensor(w_lo[:, j % 2, :], w_raw[:, j, :], w_hi[:, j % 2, :].bitcast(F32),
                                       ALU.subtract).then_inc(w_split, 1)

            def low_operands(b, i, h):
                r0, r1, par = HD * (h % 2), HD * (1 - h % 2), h % 2
                w, k1 = (W0, 2 * TB + DEC) if b == 0 else (TB, 2 * TB)
                hp = head_tile(i, h)
                qh = q[r0:r0 + HD, hp, 0:w].rearrange("p a n -> p (a n)")
                high = q_hi_of[par][r0:r0 + HD, 0:w].bitcast(F32)
                pool.wait_ge(qk_high, i * 2 + (H * b + h + 1))
                pool.tensor_tensor(tick[r0:r0 + 32, 1:2], tick[r0:r0 + 32, 0:1], tick[r0:r0 + 32, 0:1], ALU.add)
                for o in (0, HD):
                    pool.tensor_tensor(q_lo_of[par][o:o + HD, 0:w], qh, high, ALU.subtract)
                pool.tensor_tensor(k_of[par][r1:r1 + HD, 0:k1],
                                   kT[r0:r0 + HD, hp, 0:k1].rearrange("p a n -> p (a n)"),
                                   k_of[par][r0:r0 + HD, 0:k1].bitcast(F32), ALU.subtract).then_inc(qk_low, 1)

            QUADS, IN_QUADS = UNITS // 4, U_IN // 4
            for b in range(NB):
                if b == 0:
                    split(0, first=True)
                    pool.wait_ge(bias_in, 16)
                    pool.memset(bias[0:CHUNK, :, NEAR - CHUNK:NEAR], NEG)
                with pool.Fori(QUADS * b + (b == 0), QUADS * b + IN_QUADS) as i:
                    split(i)
                pool.wait_ge(w_split, UNITS * b + U_IN)
                low_operands(b, 0, 0)
                pool.wait_ge(qk_low, H * b + 1)
                split(QUADS * b + IN_QUADS, js=(0, 1))
                pool.wait_ge(w_split, UNITS * b + U_IN + 2)
                low_operands(b, 0, 1)
                low_operands(b, 0, 2)
                pool.wait_ge(qk_low, H * b + 3)
                pool.wait_ge(conv_rstd, 4 * (b + 1))
                for k in range(FT):
                    for c0, c1, s in parts(b):
                        yp = y_part(k, c0, c1, s)
                        last = pool.tensor_tensor(yp, yp, rstd[:, c0:c1], ALU.mult)
                    last.then_inc(y_scaled, 1)
                pool.wait_ge(y_scaled, FT * (b + 1))
                low_operands(b, 0, 3)
                with pool.Fori(1, H // 2 - 1) as i:
                    low_operands(b, i, 2)
                    low_operands(b, i, 3)
                pool.wait_ge(qk_low, H * (b + 1))
                split(QUADS * b + IN_QUADS, js=(2, 3))
                with pool.Fori(QUADS * b + IN_QUADS + 1, QUADS * (b + 1)) as i:
                    split(i)

        @block.tensor
        def _(pe):
            pe.wait_ge(setup_pool, 1)
            stage_no = [0]

            def enter():
                if stage_no[0]:
                    pe.wait_ge(st_act, stage_no[0])
                    pe.wait_ge(st_dve, stage_no[0])

            def leave():
                pe.drain().then_inc(st_pe, 1)
                stage_no[0] += 1

            def linear(b, u0, quads, hi, lo, kt, freed, freed_base, ready, ready_base, gates=None, between=None):
                def quad(i):
                    for j in range(4):
                        pe.wait_ge(w_split, i * 4 + (u0 + j + 1))
                        pe.wait_ge(freed, i * 4 + (freed_base + j + 1))
                        if gates is not None and j % 2 == 0:
                            pe.wait_ge(dve_freed, gates + j + 2)
                        for c0, c1, group in halves_of(b):
                            out = bank[group + j][:, 0:c1 - c0]
                            for k in range(kt):
                                wh = w_hi[:, j % 2, k * P:(k + 1) * P]
                                wl = w_lo[:, j % 2, k * P:(k + 1) * P]
                                if j == 0 and c0 == 0:
                                    pe.wait_ge(ready, ready_base + k + 1)
                                pe.matmul(out, wh, hi[:, k, c0:c1], start=(k == 0), stop=False)
                                pe.matmul(out, wh, lo[:, k, c0:c1], start=False, stop=False)
                                last = pe.matmul(out, wl, hi[:, k, c0:c1], start=False, stop=(k == kt - 1))
                        last.then_inc(unit_done, 1)
                        if between and isinstance(i, int) and j == 0:
                            between()

                if between:
                    quad(0)
                with pe.Fori(1 if between else 0, quads) as i:
                    quad(i)

            def project(b, stage, hi, lo, kt, quads, ready, ready_base, between=None):
                linear(b, unit_base(b, stage), quads, hi, lo, kt, dve_freed, dve_evac_base(b, stage),
                       ready, ready_base, between=between)

            def column_sum(b, ones, main, sample):
                for c0, c1, s in parts(b):
                    last = pe.matmul((sample if s else main)[:, 0:c1 - c0], ones[:, :], rstd[:, c0:c1],
                                     start=True, stop=True)
                return last

            leave()

            n_io = 0
            for b in range(NB):
                if b == 0:
                    enter()
                pe.wait_ge(diag_ready, b + 1)
                for t in range(n_pairs(b)):
                    n = tokens(t)
                    out = bank[0][:, t * P:(t + 1) * P] if t < NPAIR else bank[1][:, 0:DEC]
                    dg = tmp[0:n, 0, t * P:(t + 1) * P] if t < NPAIR else tmp[0:DEC, 1, 0:DEC]
                    last = pe.matmul(out, ones_d[0:n, :], dg, start=True, stop=True)
                last.then_inc(rstd_spread, 1)
                for t in range(n_pairs(b)):
                    n_tok = tokens(t)
                    pe.wait_ge(x_landed[t], 16 * (b + 1) if t < NPAIR else 16)
                    for half in range(2):
                        if n_io >= 2:
                            pe.wait_ge(io_dve if half else io_act, n_io - 1)
                        for n in range(4):
                            k = 4 * half + n
                            last = pe.transpose(io_bank[n_io % 2][half][:, n * P:n * P + n_tok],
                                                input_tile(t)[0:n_tok, k * P:(k + 1) * P],
                                                ident[0:n_tok, 0:n_tok])
                        last.then_inc(io_turned, 1)
                    n_io += 1

                if b == 0:
                    pe.wait_ge(cache_k_in, 16)
                    pe.wait_ge(io_act, n_io)
                    pe.wait_ge(io_dve, n_io)
                    for t in range(FT):
                        if t >= 2:
                            pe.wait_ge(cache_turned, t - 1)
                        for n in range(NPAIR):
                            last = pe.transpose(t_bank[t % 2][:, n * P:(n + 1) * P], o_tok[:, n, t * P:(t + 1) * P],
                                                ident[:, :])
                        last.then_inc(cache_turned_pe, 1)
                    pe.wait_ge(cache_turned, FT)
                project(b, "w_in", a_hi, a_lo, KD, 2, a_low, low_base(b, "w_in"))
                linear(b, unit_base(b, "w_in") + 8, 3, a_hi, a_lo, KD, act_freed, 12 * b,
                       a_low, low_base(b, "w_in"), gates=4 + dve_evac_base(b, "w_in") + 4)
                pe.wait_ge(act_freed, 4 + 12 * (b + 1))
                for t in range(FT):
                    if t >= 2:
                        pe.wait_ge(v_turned, FT * b + t - 1)
                    for n in range(NPAIR):
                        last = pe.transpose(t_bank[t % 2][:, n * P:(n + 1) * P], probs[:, t, n * P:(n + 1) * P],
                                            ident[:, :])
                    if b == 0:
                        last = pe.transpose(bank[6 + t % 2][0:DEC, 0:P], probs[:, t, TB:W0], ident[:, :])
                    last.then_inc(v_turned_pe, 1)
                npair = n_pairs(b)

                def score(i, h, p):
                    pair = i * (2 * npair) + (pairs_before(b) + h * npair + p)
                    par = h % 2
                    if p == 0:
                        pe.wait_ge(qk_low, i * 2 + (H * b + h + 1))
                    pe.wait_ge(shift_ready, pair + 1)
                    h2, p2 = (h, p - 2) if p >= 2 else (h - 1, p - 2 + npair)
                    if p2 in far_pairs(b) and (p >= 2 or h or not isinstance(i, int)):
                        pe.wait_ge(far_exp, i * (2 * len(far_pairs(b))) + (fars_before(b, h2, p2) + 1))
                    s = 2 * pair_slot(b, h, p)
                    if p == NPAIR:
                        runs = [(s, 0, FAR, TB), (s + 1, 0, P + DEC, TB + FAR)]
                        c0 = TB
                    else:
                        c0 = p * P
                        runs = []
                        for j in band_tiles(b, p):
                            bk, col = (s, j * P) if j < 3 else (s + 1, (j - 3) * P)
                            key = phys(b, p + j) * P
                            if runs and runs[-1][0] == bk and runs[-1][3] + col - runs[-1][1] == key:
                                runs[-1] = (bk, runs[-1][1], col + P, runs[-1][3])
                            else:
                                runs.append((bk, col, col + P, key))
                    for bk, o0, o1, key in runs:
                        masked = p < NPAIR and bk == s and o0 == 0
                        kk = k_of[par][:, key:key + o1 - o0]
                        pe.matmul(bank[bk][:, o0:o1], q_hi_of[par][:, c0:c0 + P], kk, start=True, stop=False)
                        last = pe.matmul(bank[bk][:, o0:o1], q_lo_of[par][:, c0:c0 + P], kk, start=False,
                                         stop=not masked)
                        if masked:
                            last = pe.matmul(bank[bk][:, 0:CHUNK], mask_q[:, :], mask_k[:, :],
                                             start=False, stop=True)
                    last.then_inc(scores, 1)

                def turn(i, h, p):
                    pair = i * (2 * npair) + (pairs_before(b) + h * npair + p)
                    far = i * (2 * len(far_pairs(b))) + fars_before(b, h, p)
                    pe.wait_ge(exp_done, pair + 1)
                    for tiles, tb, copied, n, turned in ((tile_parts(b, p)[0], far_bank, far_copied, far, far_turned),
                                                         (tile_parts(b, p)[1], near_bank, near_copied, pair,
                                                          near_turned)):
                        if tiles:
                            pe.wait_ge(copied, n + 1)
                            for j, keys in tiles:
                                last = pe.transpose(tb[0:keys, (j % 3) * P:(j % 3 + 1) * P],
                                                    probs[:, p, j * P:j * P + keys], ident[:, :])
                            last.then_inc(turned, 1)

                def weigh(i, h, p, first=False):
                    pair = i * (2 * npair) + (pairs_before(b) + h * npair + p)
                    far, near = tile_parts(b, p)
                    if p == 0 and first:
                        pe.wait_ge(root_ready, 2 * b + 1)
                    if p == 0:
                        pe.wait_ge(o_done, i * 2 + (H * b + h + 1))
                    if far:
                        pe.wait_ge(far_copied, i * (2 * len(far_pairs(b))) + (fars_before(b, h, p) + 2))
                    pe.wait_ge(near_copied, pair + 2)
                    for j, keys in far + near:
                        tile = phys(b, p + j) if p < NPAIR else NPAIR + j
                        last = pe.matmul(o_bank[h % 2][:, p * HD:(p + 1) * HD],
                                         pT[0:keys, pair_slot(b, h, p), j * P:(j + 1) * P],
                                         v[0:keys, tile, bass.ds(i * P + h * HD, HD)],
                                         start=(j, keys) == (far + near)[0], stop=(j, keys) == near[-1])
                    if p == npair - 1:
                        last.then_inc(pv_done, 1)

                def step(i, h, first=False, second=False, ending=False, last=False):
                    for p in range(npair):
                        if p + 2 < npair:
                            score(i, h, p + 2)
                        elif not last:
                            score(i, h + 1, p + 2 - npair)
                        turn(i, h, p)
                        if p:
                            weigh(i, h, p - 1, first)
                        elif not first:
                            weigh(i, h - 1, npair - 1)

                if b == 0:
                    pe.wait_ge(cache_v_in, 16)
                pe.wait_ge(v_turned, FT * (b + 1))
                score(0, 0, 0)
                score(0, 0, 1)
                pe.wait_ge(y_sum, b + 1)
                column_sum(b, ones_c, o_bank[0], o_bank[1]).then_inc(mean_ready, 1)
                pe.wait_ge(sq_used, 2 + squares_base(b, "conv") + FT)
                column_sum(b, ones_c, o_bank[0], o_bank[1]).then_inc(summed, 1)
                attend(pe, step)
                weigh(H // 2 - 2, 3, npair - 1)
                leave()

                if b in CUT:
                    enter()
                    first, n_tok, n_t = (2 * TB, DEC, 1) if b == 0 else ((b % 2) * TB, P, NPAIR)
                    done = FT if b == 0 else FT + 2
                    for t in range(n_t):
                        if t >= 1:
                            pe.wait_ge(cache_turned, done + t)
                        for f in range(FT):
                            last = pe.transpose(t_bank[0][0:n_tok, f * P:(f + 1) * P],
                                                kT[:, f, first + t * P:first + t * P + n_tok], ident[:, :])
                        last.then_inc(cache_turned_pe, 1)
                    for f in range(FT):
                        last = pe.transpose(t_bank[1][0:PAST, f * P:(f + 1) * P],
                                            (tail_s if b == 0 else tail)[:, f, :], ident[:, :])
                    last.then_inc(cache_turned_pe, 1)
                    leave()

                enter()
                for f in range(FT):
                    for p in range(NPAIR):
                        last = pe.transpose(bank[4 + f][:, p * P:(p + 1) * P], o_tok[:, p, f * P:(f + 1) * P],
                                            ident[:, :])
                    if b == 0:
                        last = pe.transpose(bank[f][:, 0:DEC], o_tok[0:DEC, NPAIR, f * P:(f + 1) * P],
                                            ident[0:DEC, 0:DEC])
                    last.then_inc(o_turned, 1)
                project(b, "w_out", a_hi, a_lo, KD, 2, a_low, low_base(b, "w_out"))

                def ffn_norm():
                    pe.wait_ge(sq_used, 2 + squares_base(b, "w_out") + KD)
                    column_sum(b, ones_d, bank[6], bank[7]).then_inc(summed, 1)

                if b == 0:
                    ffn_norm()
                    pe.wait_ge(root_ready, 2)
                for c, nf in enumerate(F_CHUNKS):
                    project(b, f"gate_up{c}", f_hi, f_lo, KD, nf // 2, a_low, low_base(b, "gate_up"),
                            between=ffn_norm if b and c == 0 else None)
                    project(b, f"down{c}", a_hi, a_lo, nf, 2, prod_low, prod_base(b, c))

                pe.wait_ge(sq_used, 2 + squares_base(b, "down") + KD)
                for t in range(n_pairs(b)):
                    n = tokens(t)
                    last = pe.matmul(bank[2][0:n, 2 * t:2 * t + 2], rstd[:, t * P:t * P + n], ones_d[:, 0:2],
                                     start=True, stop=True)
                last.then_inc(out_summed, 1)
                for t in range(n_pairs(b)):
                    n_tok = tokens(t)
                    for half in range(2):
                        pe.wait_ge(x_gained, KD * b + 4 * half + 4)
                        pe.wait_ge(io_dve if half else io_act, n_io - 1)
                        for n in range(4):
                            k = 4 * half + n
                            last = pe.transpose(io_bank[n_io % 2][half][0:n_tok, n * P:(n + 1) * P],
                                                x[:, k, t * P:t * P + n_tok], ident[:, :])
                        last.then_inc(io_turned, 1)
                    n_io += 1

        @block.scalar
        def _(act):
            stage_no = [0]

            def fetch(b):
                for t in range(n_pairs(b)):
                    src = x_prompt[b * TB + t * P:b * TB + (t + 1) * P, :] if t < NPAIR else x_sample
                    act.dma_start(input_tile(t), src).then_inc(x_landed[t], 16)

            fetch(0)
            act.wait_ge(small_in, 16)
            act.wait_ge(setup_pool, 1)
            act.activation(credit[:, 6:7], cst[:, 0:1], ACT.Copy).then_inc(act_freed, 4)
            act.activation(credit[:, 5:6], cst[:, 0:1], ACT.Copy).then_inc(far_copied, 1)

            def enter():
                if stage_no[0]:
                    act.wait_ge(st_pe, stage_no[0])
                    act.wait_ge(st_dve, stage_no[0])

            def leave():
                act.drain().then_inc(st_act, 1)
                stage_no[0] += 1

            def input_norms(b):
                junk = tmp[:, :, :].rearrange("p a n -> p (a n)")[:, 0:D]
                done = sum(n_pairs(i) for i in range(b))
                for t in range(n_pairs(b)):
                    n = tokens(t)
                    act.wait_ge(x_landed[t], 16 * (b + 1) if t < NPAIR else 16)
                    act.activation(junk[0:n, :], input_tile(t)[0:n, :], ACT.Square,
                                   accum_out=rms_in[0:n, t:t + 1]).then_inc(act_chain, 1)
                    act.wait_ge(act_chain, done + t + 1)
                if b == 0:
                    act.activation(rms_in[0:DEC, NPAIR:], rms_in[0:DEC, NPAIR:], ACT.Sqrt, bias=RMS_EPS, scale=1.0 / D)
                act.activation(rms_in[:, 0:NPAIR], rms_in[:, 0:NPAIR], ACT.Sqrt, bias=RMS_EPS,
                               scale=1.0 / D).then_inc(col_root, 1)

            leave()
            input_norms(0)

            cached = FT
            n_cache_out = 2
            n_io = 0
            for b in range(NB):
                for t in range(n_pairs(b)):
                    n_tok = tokens(t)
                    act.wait_ge(io_turned, 2 * n_io + 1)
                    act.activation(x[:, 0:4, t * P:t * P + n_tok],
                                   io_bank[n_io % 2][0][:, :].rearrange("p (k n) -> p k n", k=4)[:, :, 0:n_tok],
                                   ACT.Copy).then_inc(io_act, 1)
                    n_io += 1

                if b == 0:
                    for t in range(FT):
                        act.wait_ge(cache_turned_pe, t + 1)
                        act.activation(kT[:, t, TB:2 * TB], t_bank[t % 2][:, :], ACT.Copy).then_inc(cache_turned, 1)

                def split_high():
                    for k in range(KD):
                        act.wait_ge(scaled, KD * b + k + 1)
                        act.activation(a_hi[:, k, 0:width(b)], tmp[:, k % 2, 0:width(b)],
                                       ACT.Copy).then_inc(high_ready, 1)

                def root(main, sample, eps):
                    for c0, c1, s in parts(b):
                        last = act.activation(rstd[:, c0:c1], (sample if s else main)[:, 0:c1 - c0], ACT.Sqrt,
                                              bias=eps)
                    last.then_inc(root_ready, 1)

                split_high()
                u0 = unit_base(b, "w_in")
                for c in range(FT):
                    act.wait_ge(unit_done, u0 + 2 * c + 2)
                    if c >= 2:
                        act.wait_ge(dve_freed, 4 + dve_evac_base(b, "w_in") + 2 * (c - 1))
                    for c0, c1, group in halves_of(b):
                        last = act.activation(tmp[:, c % 2, c0:c1],
                                              bank[group + (2 * c + 1) % 4][:, 0:c1 - c0], ACT.Sigmoid)
                    last.then_inc(gate_ready, 1)
                def qk_operands(i, h):
                    r0, par, hp = HD * (h % 2), h % 2, head_tile(i, h)
                    qh = q[r0:r0 + HD, hp, 0:width(b)].rearrange("p a n -> p (a n)")
                    for o in (0, HD):
                        act.activation(q_hi_of[par][o:o + HD, 0:width(b)], qh, ACT.Copy)
                    act.activation(k_of[par][r0:r0 + HD, 0:k1], kT[r0:r0 + HD, hp, 0:k1].rearrange("p a n -> p (a n)"),
                                   ACT.Copy).then_inc(qk_high, 1)

                k1 = 2 * TB + DEC if b == 0 else 2 * TB
                for n in range(3):
                    if n == 2:
                        act.wait_ge(act_freed, 4 + 12 * b + 8)
                        qk_operands(0, 0)
                    for t in range(FT):
                        act.wait_ge(unit_done, u0 + 8 + 4 * n + t + 1)
                        for c0, c1, group, off, s in pieces_of(b):
                            src = bank[group + t][:, off:off + c1 - c0]
                            if n == 0:
                                last = act.activation(q[:, t, c0:c1], src, ACT.Copy, scale=Q_SCALE)
                            elif n == 1:
                                k0 = 2 * TB if s else (b % 2) * TB + c0
                                last = act.activation(kT[:, t, k0:k0 + c1 - c0], src, ACT.Copy)
                            else:
                                last = act.activation(probs[:, t, c0:c1], src, ACT.Copy)
                        last.then_inc(act_freed, 1)
                for t in range(FT):
                    act.wait_ge(v_turned_pe, FT * b + t + 1)
                    if b == 0:
                        act.activation(v[0:DEC, 2 * NPAIR, t * P:(t + 1) * P],
                                       bank[6 + t % 2][0:DEC, 0:P], ACT.Copy)
                    c = (b % 2) * NPAIR
                    act.activation(v[:, c:c + NPAIR, t * P:(t + 1) * P],
                                   t_bank[t % 2][:, :].rearrange("p (k n) -> p k n", k=4),
                                   ACT.Copy).then_inc(v_turned, 1)

                qk_operands(0, 1)

                npair = n_pairs(b)

                def exponentials(i, h, p):
                    act.wait_ge(shift_ready, i * (2 * npair) + (pairs_before(b) + h * npair + p + 3))
                    s, par = 2 * pair_slot(b, h, p), h % 2
                    r, far0, near0, near1 = P, 0, 0, BANDW
                    if p == NPAIR:
                        r, near1 = DEC, TB + DEC
                    else:
                        far0, near0 = band_tiles(b, p)[0] * P, max(band_tiles(b, p)[0] - 3, 0) * P
                    if p in far_pairs(b):
                        act.activation(probs[0:r, p, far0:FAR], bank[s][0:r, far0:FAR], ACT.Exp,
                                       bias=shift[0:r, p, 2:3],
                                       accum_out=sums[0:r, par, 0, p:p + 1]).then_inc(far_exp, 1)
                    near = probs[0:r, p, FAR + near0:near1]
                    act.activation(near, near, ACT.Exp, bias=shift[0:r, p, 3:4],
                                   accum_out=sums[0:r, par, 1, p:p + 1]).then_inc(exp_done, 1)

                exponentials(0, 0, 0)
                exponentials(0, 0, 1)

                for k in range(FT):
                    act.wait_ge(centred, FT * b + k + 1)
                    act.wait_ge(sq_used, squares_base(b, "conv") + k + 1)
                    for c0, c1, s in parts(b):
                        last = act.activation(tmp[:, k % 2, c0:c1], y_part(k, c0, c1, s), ACT.Square)
                    last.then_inc(sq_ready, 1)
                act.wait_ge(summed, 2 * b + 1)
                root(o_bank[0], o_bank[1], LN_EPS)
                def copy_far(i, h, p):
                    if p in far_pairs(b):
                        act.wait_ge(far_turned, i * (2 * len(far_pairs(b))) + (fars_before(b, h, p) + 1))
                        c0 = tile_parts(b, p)[0][0][0] * P
                        act.activation(pT[:, pair_slot(b, h, p), c0:FAR], far_bank[:, c0:FAR],
                                       ACT.Copy).then_inc(far_copied, 1)

                def normed_swish():
                    for k in range(FT):
                        act.wait_ge(y_scaled, FT * b + k + 1)
                        for c0, c1, s in parts(b):
                            yp = y_part(k, c0, c1, s)
                            act.activation(yp, yp, ACT.Silu, bias=cst[:, C_LNB + k:C_LNB + k + 1],
                                           scale=cst[:, C_LNG + k:C_LNG + k + 1])

                def step(i, h, first=False, second=False, ending=False, last=False):
                    for p in range(npair):
                        if not first or p >= 2:
                            exponentials(i, h, p)
                        if p:
                            copy_far(i, h, p - 1)
                        elif not first:
                            copy_far(i, h - 1, npair - 1)
                    if not ending:
                        qk_operands(i, h + 2)

                attend(act, step)
                copy_far(H // 2 - 2, 3, npair - 1)
                normed_swish()
                leave()

                if b in CUT:
                    enter()
                    n_tok, n_t = (DEC, 1) if b == 0 else (P, NPAIR)
                    nk, nv, ncv = (nk_sample, nv_sample, nc_sample) if b == 0 else (nk_prompt, nv_prompt, nc_prompt)
                    r0 = TB - DEC if b == 0 else 0
                    for t in range(n_t):
                        act.wait_ge(cache_turned_pe, cached + 1)
                        dst = rows[0:n_tok, t // 2, (t % 2) * AW:(t % 2 + 1) * AW]
                        act.activation(dst, t_bank[0][0:n_tok, :], ACT.Copy).then_inc(cache_turned, 1)
                        cached += 1
                        act.wait_ge(cache_turned, cached)
                        act.dma_start(nk[r0 + t * P:r0 + t * P + n_tok, :], dst).then_inc(cache_out, 16)
                    act.wait_ge(cache_turned_pe, cached + 1)
                    dst = x_in[0:PAST, 0, 0:AW] if b else rows[0:PAST, 1, 0:AW]
                    act.activation(dst, t_bank[1][0:PAST, :], ACT.Copy).then_inc(cache_turned, 1)
                    cached += 1
                    act.wait_ge(cache_turned, cached)
                    act.dma_start(ncv, dst).then_inc(cache_out, 16)
                    if b == 0:
                        act.dma_start(nv[r0:r0 + DEC, :], v[0:DEC, 2 * NPAIR, :]).then_inc(cache_out, 16)
                    else:
                        c = (b % 2) * NPAIR
                        act.dma_start(nv.rearrange("(t p) n -> p t n", p=P),
                                      v[:, c:c + NPAIR, :]).then_inc(cache_out, 16)
                    n_cache_out += n_t + 2
                    leave()

                enter()
                if b + 1 < NB:
                    fetch(b + 1)
                for k in range(FT):
                    act.wait_ge(o_turned, FT * b + k + 1)
                    if b == 0:
                        act.activation(a_hi[:, k, TB:W0], bank[k][:, 0:DEC], ACT.Copy)
                    act.activation(a_hi[:, k, 0:TB], bank[4 + k][:, :], ACT.Copy).then_inc(high_ready, 1)
                for k in range(FT):
                    for c0, c1, s in parts(b):
                        last = act.activation(a_hi[:, FT + k, c0:c1], y_part(k, c0, c1, s), ACT.Copy)
                    last.then_inc(high_ready, 1)

                def squares(stage, part):
                    with act.Fori(0, 2) as i:
                        for j in range(4):
                            act.wait_ge(dve_freed, i * 4 + (4 + dve_evac_base(b, stage) + j + 1))
                            n = bass.ds(i * 4 + j, 1)
                            xt = x[:, n, 0:width(b)].rearrange("p a n -> p (a n)")
                            act.wait_ge(sq_used, i * 4 + (squares_base(b, part) + j + 1))
                            act.activation(tmp[:, j % 2, 0:width(b)], xt, ACT.Square).then_inc(sq_ready, 1)
                            if part == "w_out":
                                act.activation(f_hi[:, n, 0:width(b)].rearrange("p a n -> p (a n)"), xt, ACT.Copy,
                                               scale=cst[:, bass.ds(i * 4 + (C_GFFN + j), 1)]
                                               ).then_inc(high_ready, 1)
                            if part == "down":
                                act.activation(xt, xt, ACT.Copy, scale=cst[:, bass.ds(i * 4 + (C_GFIN + j), 1)]
                                               ).then_inc(x_gained, 1)

                squares("w_out", "w_out")
                if b in CUT:
                    act.wait_ge(cache_out, 16 * n_cache_out)
                act.wait_ge(summed, 2 * b + 2)
                root(bank[6], bank[7], RMS_EPS)
                for c, nf in enumerate(F_CHUNKS):
                    with act.Fori(0, nf // 2) as i:
                        for j in range(2):
                            act.wait_ge(gate_scaled, i * 2 + (prod_base(b, c) + j + 1))
                            t = tmp[:, j, 0:width(b)]
                            act.activation(t, t, ACT.Silu).then_inc(gate_ready, 1)
                            act.wait_ge(dve_freed, i * 4 + (4 + dve_evac_base(b, f"gate_up{c}") + 2 * j + 2))
                            act.activation(a_hi[:, bass.ds(i * 2 + j, 1), 0:width(b)].rearrange("p a n -> p (a n)"),
                                           t, ACT.Copy).then_inc(prod_high, 1)
                    if c == 1 and b + 1 < NB:
                        act.wait_ge(prod_low, prod_base(b, 2))
                        input_norms(b + 1)
                squares(f"down{len(F_CHUNKS) - 1}", "down")

                act.wait_ge(out_summed, b + 1)
                if b == 0:
                    act.activation(rms_out[0:DEC, 2 * NPAIR:], bank[2][0:DEC, 8:10], ACT.Sqrt, bias=RMS_EPS)
                act.activation(rms_out[:, 0:2 * NPAIR], bank[2][:, 0:8], ACT.Sqrt, bias=RMS_EPS).then_inc(out_root, 1)
                act.wait_ge(out_rstd, b + 1)

                def send(t, n):
                    act.wait_ge(io_act, n + 1)
                    act.wait_ge(io_dve, n + 1)
                    dst = y_prompt[b * TB + t * P:b * TB + (t + 1) * P, :] if t < NPAIR else y_sample
                    act.dma_start(dst, rows[0:tokens(t), t % NPAIR, :]).then_inc(out_landed[t], 16)

                for t in range(n_pairs(b)):
                    n_tok = tokens(t)
                    if t == NPAIR:
                        send(NPAIR - 1, n_io - 1)
                        act.wait_ge(out_landed[0], 16 * (b + 1))
                    act.wait_ge(io_turned, 2 * n_io + 1)
                    act.activation(rows[0:n_tok, t % NPAIR, 0:512], io_bank[n_io % 2][0][0:n_tok, :], ACT.Copy,
                                   scale=rms_out[0:n_tok, 2 * t:2 * t + 1]).then_inc(io_act, 1)
                    if 0 < t < NPAIR:
                        send(t - 1, n_io - 1)
                    n_io += 1
                send(n_pairs(b) - 1, n_io - 1)
            for t in range(NPAIR):
                act.wait_ge(out_landed[t], 16 * NB)
            act.wait_ge(out_landed[NPAIR], 16)

        @block.vector
        def _(dve):
            stage_no = [0]
            made = [0]

            def link(ins, at=None, lag=0):
                ins.then_inc(chain, 1)
                made[0] += 1
                dve.wait_ge(chain, made[0] - lag if at is None else at + (made[0] - lag))

            def enter():
                if stage_no[0]:
                    dve.wait_ge(st_pe, stage_no[0])
                    dve.wait_ge(st_act, stage_no[0])

            def leave():
                dve.drain().then_inc(st_dve, 1)
                stage_no[0] += 1

            dve.memset(sums[:, :, :, :], 0.0)
            dve.memset(tail[:, :, :], 0.0).then_inc(dve_freed, 4)
            dve.memset(credit[:, 3:4], 0.0).then_inc(near_copied, 1)
            dve.memset(credit[:, 4:5], 0.0).then_inc(shift_ready, 2)
            dve.memset(credit[:, 2:3], 0.0).then_inc(o_done, 2)
            dve.wait_ge(small_in, 16)
            dve.memset(credit[:, 1:2], 0.0).then_inc(sq_used, 2)
            leave()
            n_io = 0
            highs = 0

            def input_diagonals(b):
                dve.wait_ge(col_root, b + 1)
                if b == 0:
                    dve.reciprocal(rms_in[0:DEC, NPAIR:], rms_in[0:DEC, NPAIR:])
                link(dve.reciprocal(rms_in[:, 0:NPAIR], rms_in[:, 0:NPAIR]))
                if b == 0:
                    dve.tensor_scalar(tmp[0:DEC, 1, 0:DEC], ident[0:DEC, 0:DEC], rms_in[0:DEC, NPAIR:], None, ALU.mult)
                for t in range(NPAIR):
                    last = dve.tensor_scalar(tmp[:, 0, t * P:(t + 1) * P], ident[:, :], rms_in[:, t:t + 1],
                                             None, ALU.mult)
                last.then_inc(diag_ready, 1)

            input_diagonals(0)
            for b in range(NB):
                w = width(b)
                dve.wait_ge(rstd_spread, b + 1)
                for c0, c1, s in parts(b):
                    last = dve.tensor_scalar(rstd[:, c0:c1], bank[1 if s else 0][:, 0:c1 - c0], float(D), None,
                                             ALU.mult)
                link(last)
                for t in range(n_pairs(b)):
                    n_tok = tokens(t)
                    dve.wait_ge(io_turned, 2 * n_io + 2)
                    dve.tensor_copy(x[:, 4:8, t * P:t * P + n_tok],
                                    io_bank[n_io % 2][1][:, :].rearrange("p (k n) -> p k n", k=4)[:, :, 0:n_tok]
                                    ).then_inc(io_dve, 1)
                    n_io += 1

                def split_low(k, src):
                    nonlocal highs
                    highs += 1
                    dve.wait_ge(high_ready, highs)
                    for c0, c1, ap in src:
                        last = dve.tensor_tensor(a_lo[:, k, c0:c1], ap, a_hi[:, k, c0:c1].bitcast(F32), ALU.subtract)
                    last.then_inc(a_low, 1)

                def scale_and_split():

                    def scale_tile(k):
                        dve.scalar_tensor_tensor(out=tmp[:, k % 2, 0:w], in0=x[:, k, 0:w],
                                                 scalar=cst[:, C_GMIX + k:C_GMIX + k + 1],
                                                 in1=rstd[:, 0:w], op0=ALU.mult, op1=ALU.mult).then_inc(scaled, 1)

                    scale_tile(0)
                    for k in range(KD):
                        if k + 1 < KD:
                            if k >= 1:
                                dve.wait_ge(a_low, low_base(b, "w_in") + k)
                            scale_tile(k + 1)
                        split_low(k, [(0, w, tmp[:, k % 2, 0:w])])

                dve.wait_ge(io_act, n_io)
                dve.wait_ge(io_dve, n_io)
                scale_and_split()

                if b:
                    for t in range(n_pairs(b - 1)):
                        dve.wait_ge(out_landed[t], 16 * b if t < NPAIR else 16)
                YWb = YW if b == 0 else TB
                dve.tensor_copy(u[:, :, 0:PAST], tail[:, :, :])
                if b == 0:
                    dve.tensor_copy(u[:, :, PAST + TB:2 * PAST + TB],
                                    cst[:, C_PAST:C_ALL].rearrange("p (c n) -> p c n", c=FT))

                def gate(c):
                    dve.wait_ge(gate_ready, gate_base(b, 0) - FT + c + 1)
                    for c0, c1, group, off, s in pieces_of(b):
                        o = c0 + (2 * PAST if s else PAST)
                        last = dve.tensor_tensor(u[:, c, o:o + c1 - c0],
                                                 bank[group + (2 * c) % 4][:, off:off + c1 - c0],
                                                 tmp[:, c % 2, c0:c1], ALU.mult)
                    last.then_inc(dve_freed, 2)

                def first_tap(c):
                    dve.tensor_scalar(y[:, c, 0:YWb], u[:, c, 0:YWb],
                                      cst[:, C_WDW + c * TAPS:C_WDW + c * TAPS + 1],
                                      cst[:, C_BDW + c:C_BDW + c + 1], ALU.mult, ALU.add).then_inc(chain, 1)
                    made[0] += 1

                def taps(c0, turn0, turn1):
                    n0 = made[0]
                    with dve.Fori(turn0, turn1) as i:
                        for s in range(6):
                            for c in range(2):
                                dve.wait_ge(chain, i * 12 + (n0 - 12 * turn0 + s * 2 + c - 1))
                                dve.scalar_tensor_tensor(
                                    out=y[:, c0 + c, 0:YWb], in0=u[:, c0 + c, bass.ds(i * 6 + (s + 1), YWb)],
                                    scalar=cst[:, bass.ds(i * 6 + (C_WDW + (c0 + c) * TAPS + s + 1), 1)],
                                    in1=y[:, c0 + c, 0:YWb], op0=ALU.mult, op1=ALU.add).then_inc(chain, 1)
                    made[0] += 12 * (turn1 - turn0)

                gate(0)
                gate(1)
                dve.wait_ge(dve_freed, 4 + dve_evac_base(b, "w_in") + 4)
                first_tap(0)
                first_tap(1)
                taps(0, 0, 2)
                gate(2)
                taps(0, 2, 3)
                gate(3)
                taps(0, 3, 5)
                dve.wait_ge(dve_freed, 4 + dve_evac_base(b, "w_in") + 8)
                dve.tensor_copy(tail[:, :, :], u[:, :, TB:TB + PAST])
                if b == 0:
                    dve.tensor_copy(tail_s[:, :, :], u[:, :, UW - PAST:UW])
                first_tap(2)
                first_tap(3)
                taps(2, 0, 5)
                dve.wait_ge(chain, made[0])

                for k in range(1, FT):
                    for c0, c1, s in parts(b):
                        last = dve.tensor_tensor(rstd[:, c0:c1], y_part(0, c0, c1, s) if k == 1 else rstd[:, c0:c1],
                                                 y_part(k, c0, c1, s), ALU.add)
                    if k < FT - 1:
                        link(last)
                last.then_inc(y_sum, 1)
                npair = n_pairs(b)
                per_head = shift_links(b)

                def shifts(i, h, p):
                    here = i * (2 * per_head)
                    dve.wait_ge(scores, i * (2 * npair) + (pairs_before(b) + h * npair + p + 1))
                    s = 2 * pair_slot(b, h, p)
                    if p == NPAIR:
                        r, far0, near0, near1 = DEC, 0, 0, P + DEC
                    else:
                        r, far0, near0, near1 = P, band_tiles(b, p)[0] * P, max(band_tiles(b, p)[0] - 3, 0) * P, NEAR
                    out = probs[0:r, p, FAR + near0:FAR + near1]
                    far_max, near_max = shift[0:r, p, 0:1], shift[0:r, p, 1:2]
                    far_shift, near_shift = shift[0:r, p, 2:3], shift[0:r, p, 3:4]
                    farb = cst[0:r, bass.ds(i * 2 + (C_FARB + h), 1)]
                    hb = bias[0:r, bass.ds(i * 2 + h, 1), near0:near1].rearrange("p a n -> p (a n)")
                    if p in far_pairs(b):
                        link(dve.tensor_tensor(out, bank[s + 1][0:r, near0:near1], hb, ALU.add), here, 1)
                        link(dve.tensor_reduce(far_max, bank[s][0:r, far0:FAR], AX_X, ALU.max, negate=True), here, 1)
                        link(dve.tensor_reduce(near_max, out, AX_X, ALU.max, negate=True), here)
                        link(dve.tensor_scalar(near_shift, far_max, farb, near_max, ALU.subtract, ALU.min), here)
                        dve.tensor_scalar(far_shift, near_shift, farb, None, ALU.add).then_inc(shift_ready, 1)
                    else:
                        link(dve.tensor_tensor(out, bank[s + 1][0:r, near0:near1], hb, ALU.add), here)
                        dve.tensor_reduce(near_shift, out, AX_X, ALU.max, negate=True).then_inc(shift_ready, 1)

                n0 = made[0]
                shifts(0, 0, 0)
                shifts(0, 0, 1)
                done = made[0] - n0
                dve.wait_ge(mean_ready, b + 1)
                if b == 0:
                    for t in (q_hi, q_lo, q_hi1, q_lo1):
                        dve.memset(t[:, W0:640].bitcast(F32), 0.0)
                for k in range(FT):
                    for c0, c1, s in parts(b):
                        yp = y_part(k, c0, c1, s)
                        last = dve.tensor_tensor(yp, yp, o_bank[int(s)][:, 0:c1 - c0], ALU.subtract)
                    last.then_inc(centred, 1)
                link(dve.memset(rstd[:, 0:w], 0.0))

                def add_square(n, slot, part, at=0):
                    n1 = squares_base(b, part) + n
                    dve.wait_ge(sq_ready, at + (n1 + 1))
                    dve.wait_ge(sq_used, at + (n1 + 2))
                    dve.tensor_tensor(rstd[:, 0:w], rstd[:, 0:w], tmp[:, slot, 0:w], ALU.add).then_inc(sq_used, 1)

                for k in range(FT):
                    add_square(k, k % 2, "conv")
                n0 = made[0] - done

                def copy_near(i, h, p):
                    dve.wait_ge(near_turned, i * (2 * npair) + (pairs_before(b) + h * npair + p + 1))
                    slot = pair_slot(b, h, p)
                    for j0, j1, keys in ([(3, 4, P), (4, 5, DEC)] if p == NPAIR else
                                         [(tile_parts(b, p)[1][0][0], 5, P)]):
                        last = dve.tensor_copy(pT[0:keys, slot, j0 * P:j1 * P],
                                               near_bank[0:keys, (j0 - 3) * P:(j1 - 3) * P])
                    last.then_inc(near_copied, 1)

                def take_output(i, h):
                    head, par = i * 2 + (H * b + h), h % 2
                    cols = bass.ds(i * P + h * HD, HD)
                    dve.wait_ge(pv_done, head + 1)
                    if b == 0:
                        dve.tensor_tensor(inverse[0:DEC, NPAIR:], sums[0:DEC, par, 0, NPAIR:],
                                          sums[0:DEC, par, 1, NPAIR:], ALU.add)
                    dve.tensor_tensor(inverse[:, 0:NPAIR], sums[:, par, 0, 0:NPAIR], sums[:, par, 1, 0:NPAIR],
                                      ALU.add).then_inc(totals, 1)
                    dve.wait_ge(totals, i * 4 + (2 * (H * b + h) + 1))
                    if b == 0:
                        dve.reciprocal(inverse[0:DEC, NPAIR:], inverse[0:DEC, NPAIR:])
                    dve.reciprocal(inverse[:, 0:NPAIR], inverse[:, 0:NPAIR]).then_inc(totals, 1)
                    dve.wait_ge(totals, i * 4 + (2 * (H * b + h) + 2))
                    for p in range(npair):
                        r = DEC if p == NPAIR else P
                        last = dve.tensor_scalar(o_tok[0:r, p, cols], o_bank[par][0:r, p * HD:(p + 1) * HD],
                                                 inverse[0:r, p:p + 1], None, ALU.mult)
                    last.then_inc(o_done, 1)

                def step(i, h, first=False, second=False, ending=False, last=False):
                    made[0] = n0 + h * per_head + (done if first else 0)
                    for p in range(npair):
                        if not first or p >= 2:
                            shifts(i, h, p)
                        if p >= 2:
                            copy_near(i, h, p - 2)
                        elif not first:
                            copy_near(i, h - 1, npair - 2 + p)
                        if p == 3 and not first:
                            take_output(i, h - 1)
                        if second and p < 4:
                            if p == 0:
                                dve.wait_ge(root_ready, 2 * b + 1)
                            part = rstd[:, p * w // 4:(p + 1) * w // 4]
                            dve.reciprocal(part, part).then_inc(conv_rstd, 1)
                    assert made[0] == n0 + (h + 1) * per_head

                attend(dve, step)
                for p in (npair - 2, npair - 1):
                    copy_near(H // 2 - 2, 3, p)
                take_output(H // 2 - 2, 3)
                made[0] = n0 + H * per_head
                leave()
                if b in CUT:
                    enter()
                    leave()

                enter()
                for k in range(FT):
                    split_low(k, [(0, TB, bank[4 + k][:, :])] + ([(TB, W0, bank[k][:, 0:DEC])] if b == 0 else []))
                for k in range(FT):
                    split_low(FT + k, [(c0, c1, y_part(k, c0, c1, s)) for c0, c1, s in parts(b)])

                def add_residual(stage, part=None):
                    u0 = unit_base(b, stage)
                    if part:
                        link(dve.memset(rstd[:, 0:w], 0.0))
                    with dve.Fori(0, 2) as i:
                        for j in range(4):
                            dve.wait_ge(unit_done, i * 4 + (u0 + j + 1))
                            for c0, c1, group in halves_of(b):
                                xt = x[:, bass.ds(i * 4 + j, 1), c0:c1].rearrange("p a n -> p (a n)")
                                last = dve.tensor_tensor(xt, bank[group + j][:, 0:c1 - c0], xt, ALU.add)
                            last.then_inc(dve_freed, 1)
                            if part == "w_out":
                                n = bass.ds(i * 4 + j, 1)
                                dve.wait_ge(high_ready, i * 4 + (highs + j + 1))
                                dve.scalar_tensor_tensor(
                                    out=f_lo[:, n, 0:w].rearrange("p a n -> p (a n)"),
                                    in0=x[:, n, 0:w].rearrange("p a n -> p (a n)"),
                                    scalar=cst[:, bass.ds(i * 4 + (C_GFFN + j), 1)],
                                    in1=f_hi[:, n, 0:w].rearrange("p a n -> p (a n)").bitcast(F32),
                                    op0=ALU.mult, op1=ALU.subtract).then_inc(a_low, 1)
                            if part:
                                add_square(j, j % 2, part, i * 4)

                add_residual("w_out", "w_out")
                dve.wait_ge(root_ready, 2 * b + 2)
                link(dve.reciprocal(rstd[:, 0:w], rstd[:, 0:w]))
                highs += KD
                for c, nf in enumerate(F_CHUNKS):
                    if c == 2 and b + 1 < NB:
                        dve.wait_ge(col_root, b + 2)
                    u0 = unit_base(b, f"gate_up{c}")
                    with dve.Fori(0, nf // 2) as i:
                        for j in range(2):
                            n = i * 2 + (prod_base(b, c) + j + 1)
                            t, f = tmp[:, j, 0:w], bass.ds(i * 2 + j, 1)
                            dve.wait_ge(unit_done, i * 4 + (u0 + 2 * j + 1))
                            for c0, c1, group in halves_of(b):
                                last = dve.tensor_tensor(tmp[:, j, c0:c1], bank[group + 2 * j][:, 0:c1 - c0],
                                                         rstd[:, c0:c1], ALU.mult)
                            last.then_inc(gate_scaled, 1)
                            dve.wait_ge(gate_ready, i * 2 + (gate_base(b, c) + j + 1))
                            dve.tensor_tensor(t, t, rstd[:, 0:w], ALU.mult).then_inc(dve_freed, 1)
                            dve.wait_ge(dve_freed, i * 4 + (4 + dve_evac_base(b, f"gate_up{c}") + 2 * j + 1))
                            dve.wait_ge(unit_done, i * 4 + (u0 + 2 * j + 2))
                            for c0, c1, group in halves_of(b):
                                last = dve.tensor_tensor(tmp[:, j, c0:c1], bank[group + 2 * j + 1][:, 0:c1 - c0],
                                                         tmp[:, j, c0:c1], ALU.mult)
                            last.then_inc(dve_freed, 1)
                            dve.wait_ge(prod_high, n)
                            dve.tensor_tensor(a_lo[:, f, 0:w].rearrange("p a n -> p (a n)"), t,
                                              a_hi[:, f, 0:w].rearrange("p a n -> p (a n)").bitcast(F32),
                                              ALU.subtract).then_inc(prod_low, 1)
                    add_residual(f"down{c}", "down" if c == len(F_CHUNKS) - 1 else None)

                dve.wait_ge(out_root, b + 1)
                if b == 0:
                    dve.reciprocal(rms_out[0:DEC, 2 * NPAIR:], rms_out[0:DEC, 2 * NPAIR:])
                dve.reciprocal(rms_out[:, 0:2 * NPAIR], rms_out[:, 0:2 * NPAIR]).then_inc(out_rstd, 1)
                dve.wait_ge(out_rstd, b + 1)
                if b + 1 < NB:
                    input_diagonals(b + 1)
                for t in range(n_pairs(b)):
                    n_tok = tokens(t)
                    if t == NPAIR:
                        dve.wait_ge(out_landed[0], 16 * (b + 1))
                    dve.wait_ge(io_turned, 2 * n_io + 2)
                    dve.tensor_scalar(rows[0:n_tok, t % NPAIR, 512:D], io_bank[n_io % 2][1][0:n_tok, :],
                                      rms_out[0:n_tok, 2 * t:2 * t + 1], None, ALU.mult).then_inc(io_dve, 1)
                    n_io += 1


def shift_links(b):
    return sum(4 if p == NPAIR or band_tiles(b, p)[0] < 3 else 1 for p in range(n_pairs(b)))


def kernel(**inputs):
    import numpy as np
    import concourse.bacc as bacc
    from concourse.bass_utils import run_bass_kernel_spmd

    nc = bacc.Bacc("TRN2", target_bir_lowering=False, num_devices=1)
    a = {k: np.asarray(v_) for k, v_ in inputs.items()}

    def unit(w, n, k0=0, kt=KD):
        t = w[k0 * P:(k0 + kt) * P, n * P:(n + 1) * P].reshape(kt, P, P).transpose(1, 0, 2).reshape(P, kt * P)
        out = np.zeros((P, D), np.float32)
        out[:, :kt * P] = t
        return out

    w_in, w_out, w_g, w_u, w_d = (a[n][0] for n in ("w_in", "w_out", "w_gate", "w_up", "w_down"))
    units = []
    for c in range(FT):
        units += [unit(w_in, 3 * FT + c), unit(w_in, 4 * FT + c)]
    units += [unit(w_in, n) for n in range(3 * FT)]
    units += [unit(w_out, n) for n in range(KD)]
    f0 = 0
    for nf in F_CHUNKS:
        for f in range(f0, f0 + nf):
            units += [unit(w_g, f), unit(w_u, f)]
        units += [unit(w_d, n, f0, nf) for n in range(KD)]
        f0 += nf

    def columns(vec):
        return vec.reshape(-1, P).T

    table = a["rel_table"][0]
    consts = np.concatenate([
        columns(a["g_mix"][0]), columns(a["g_ffn"][0]), columns(a["g_final"]),
        columns(a["b_dw"][0]), columns(a["ln_g"][0]), columns(a["ln_b"][0]),
        np.broadcast_to(table[:, 2 * CLIP], (P, H)),
        a["w_dw"][0].reshape(TAPS, FT, P).transpose(2, 1, 0).reshape(P, FT * TAPS),
        a["state_conv"][0, 0].reshape(PAST, FT, P).transpose(2, 1, 0).reshape(P, FT * PAST),
    ], axis=1)
    distance = np.arange(P)[:, None] - np.arange(NEAR)[None, :] + P
    rel_near = table[:, np.clip(distance, -CLIP, CLIP) + CLIP].transpose(1, 0, 2)

    arrays = {
        "w_units": np.stack(units),
        "x_prompt": a["x_prompt"][0], "x_sample": a["x_sample"][0],
        "cache_k": a["cache_k"].reshape(TB, AW), "cache_v": a["cache_v"].reshape(TB, AW),
        "consts": consts, "rel_near": rel_near,
    }
    arrays = {k: np.ascontiguousarray(v_) for k, v_ in arrays.items()}
    outs = {"y_prompt": (SEQ, D), "y_sample": (DEC, D), "nk_prompt": (TB, AW), "nv_prompt": (TB, AW),
            "nc_prompt": (PAST, AW), "nk_sample": (TB, AW), "nv_sample": (TB, AW), "nc_sample": (PAST, AW)}
    args = [nc.dram_tensor(k, v_.shape, F32, kind="ExternalInput").ap() for k, v_ in arrays.items()]
    args += [nc.dram_tensor(k, s, F32, kind="ExternalOutput").ap() for k, s in outs.items()]
    build(nc, *args)
    r = run_bass_kernel_spmd(nc, [arrays], core_ids=[0]).results[0]
    return (r["y_prompt"].reshape(1, SEQ, D), r["y_sample"].reshape(1, DEC, D),
            r["nk_prompt"].reshape(1, 1, TB, H, HD), r["nv_prompt"].reshape(1, 1, TB, H, HD),
            r["nc_prompt"].reshape(1, 1, PAST, AW),
            r["nk_sample"].reshape(1, 1, TB, H, HD), r["nv_sample"].reshape(1, 1, TB, H, HD),
            r["nc_sample"].reshape(1, 1, PAST, AW))
```
